# Optimizing a Trainium2 kernel written in Bass

```python
import jax
import jax.numpy as jnp
from jax import lax
import numpy as np

D_MODEL = 1024
BATCH = 1
SEQ = 256
DEPTH = 2

GRID_W = 64
CTX_LEN = 256
HEAD_DIM = 64
N_HEADS_A = 8
N_KV_A = 2
N_HEADS_B = 8
N_KV_B = 2
N_HEADS_N = 8
BRANCH_WIDTH = 8 * HEAD_DIM
N_BRANCHES = 3
Q_BLOCK = 128
WINDOW = 128
NA_ROWS = 8
NA_COLS = 16
ROPE_THETA = 10000.0
N_EXPERTS = 16
N_GROUPS = 4
EXPERTS_PER_GROUP = N_EXPERTS // N_GROUPS
TOP_K = 2
D_FF_EXPERT = 512
EPS = 1e-6
NEG_INF = -1e30
ATTN_SCALE = HEAD_DIM ** -0.5

IN_SPLITS = (N_HEADS_A * HEAD_DIM, N_KV_A * HEAD_DIM, N_KV_A * HEAD_DIM,
             N_HEADS_B * HEAD_DIM, N_KV_B * HEAD_DIM, N_KV_B * HEAD_DIM,
             N_HEADS_N * HEAD_DIM, N_HEADS_N * HEAD_DIM, N_HEADS_N * HEAD_DIM,
             N_BRANCHES * D_MODEL)
IN_COLS = sum(IN_SPLITS)
IN_OFFSETS = tuple(int(o) for o in np.cumsum(IN_SPLITS)[:-1])

kernel_name = 'hybrid_dit_parallel_attn_moe'

def _rmsnorm(x, g):
    xf = x.astype(jnp.float32)
    y = xf * lax.rsqrt(jnp.mean(xf * xf, axis=-1, keepdims=True) + EPS)
    return (y * g.astype(jnp.float32)).astype(x.dtype)

def _modulate(x, g, shift, scale):
    return _rmsnorm(x, g) * (1 + scale) + shift

def _heads(x, n):
    return x.reshape(*x.shape[:-1], n, HEAD_DIM)

def _rope_tables(S):
    t = jnp.arange(S, dtype=jnp.int32)
    row = (t // GRID_W).astype(jnp.float32)
    col = (t % GRID_W).astype(jnp.float32)
    half = HEAD_DIM // 2
    inv = ROPE_THETA ** (-jnp.arange(0, half, 2, dtype=jnp.float32) / half)
    ang = jnp.stack([row[:, None] * inv, col[:, None] * inv], axis=1)
    return jnp.cos(ang), jnp.sin(ang)

def _rope_2d(x, cos, sin):
    xr = x.reshape(*x.shape[:-1], 2, 2, HEAD_DIM // 4)
    x1, x2 = xr[..., 0, :], xr[..., 1, :]
    cs = cos[None, :, None].astype(x.dtype)
    sn = sin[None, :, None].astype(x.dtype)
    out = jnp.stack([x1 * cs - x2 * sn, x1 * sn + x2 * cs], axis=-2)
    return out.reshape(x.shape)

def _ctx_attention(q, k, v, sink=None):
    B, L, HQ, DH = q.shape
    HKV = k.shape[2]
    G = HQ // HKV
    s = jnp.einsum('bqkgd,bskd->bkgqs', q.reshape(B, L, HKV, G, DH), k).astype(jnp.float32) * ATTN_SCALE
    if sink is not None:
        s_sink = jnp.broadcast_to(sink.astype(jnp.float32).reshape(1, HKV, G, 1, 1), s.shape[:-1] + (1,))
        s = jnp.concatenate([s, s_sink], axis=-1)
    p = jax.nn.softmax(s, axis=-1)
    if sink is not None:
        p = p[..., :-1]
    o = jnp.einsum('bkgqs,bskd->bqkgd', p.astype(v.dtype), v)
    return o.reshape(B, L, HQ * DH)

def _global_attention(q, k, v, ck, cv):
    B, S, HQ, DH = q.shape
    HKV = k.shape[2]
    G = HQ // HKV
    nb = S // Q_BLOCK
    keys = jnp.concatenate([k, ck], axis=1)
    vals = jnp.concatenate([v, cv], axis=1)
    qb = q.reshape(B, nb, Q_BLOCK, HKV, G, DH).transpose(1, 0, 2, 3, 4, 5)

    def block(qi):
        s = jnp.einsum('bqkgd,bskd->bkgqs', qi, keys).astype(jnp.float32) * ATTN_SCALE
        p = jax.nn.softmax(s, axis=-1).astype(vals.dtype)
        return jnp.einsum('bkgqs,bskd->bqkgd', p, vals)

    o = lax.map(block, qb)
    return o.transpose(1, 0, 2, 3, 4, 5).reshape(B, S, HQ * DH)

def _window_attention(q, k, v, ck, cv, sink):
    B, S, HQ, DH = q.shape
    HKV = k.shape[2]
    G = HQ // HKV
    nb = S // Q_BLOCK
    L = ck.shape[1]
    span = Q_BLOCK + 2 * WINDOW
    pad = ((0, 0), (WINDOW, WINDOW), (0, 0), (0, 0))
    k_pad = jnp.pad(k, pad)
    v_pad = jnp.pad(v, pad)
    qi_idx = jnp.arange(Q_BLOCK)[:, None]
    kj_idx = jnp.arange(span)[None, :]
    band = jnp.abs(kj_idx - WINDOW - qi_idx) <= WINDOW
    sink_col = sink.astype(jnp.float32).reshape(1, HKV, G, 1, 1)
    qb = q.reshape(B, nb, Q_BLOCK, HKV, G, DH).transpose(1, 0, 2, 3, 4, 5)

    def block(args):
        i, qi = args
        start = i * Q_BLOCK
        kw = lax.dynamic_slice_in_dim(k_pad, start, span, axis=1)
        vw = lax.dynamic_slice_in_dim(v_pad, start, span, axis=1)
        kpos = start - WINDOW + kj_idx
        valid = band & (kpos >= 0) & (kpos < S)
        s_loc = jnp.einsum('bqkgd,bskd->bkgqs', qi, kw).astype(jnp.float32) * ATTN_SCALE
        s_loc = jnp.where(valid, s_loc, NEG_INF)
        s_ctx = jnp.einsum('bqkgd,bskd->bkgqs', qi, ck).astype(jnp.float32) * ATTN_SCALE
        s_sink = jnp.broadcast_to(sink_col, s_ctx.shape[:-1] + (1,))
        p = jax.nn.softmax(jnp.concatenate([s_loc, s_ctx, s_sink], axis=-1), axis=-1).astype(v.dtype)
        return (jnp.einsum('bkgqs,bskd->bqkgd', p[..., :span], vw)
                + jnp.einsum('bkgqs,bskd->bqkgd', p[..., span:span + L], cv))

    o = lax.map(block, (jnp.arange(nb, dtype=jnp.int32), qb))
    return o.transpose(1, 0, 2, 3, 4, 5).reshape(B, S, HQ * DH)

def _neighbourhood_attention(q, k, v, ck, cv, rpb, rows):
    B, S, H, DH = q.shape
    kh = min(NA_ROWS, rows)
    kw = NA_COLS
    qg = q.reshape(B, rows, GRID_W, H, DH).transpose(1, 0, 2, 3, 4)
    kg = k.reshape(B, rows, GRID_W, H, DH)
    vg = v.reshape(B, rows, GRID_W, H, DH)
    col = jnp.arange(GRID_W, dtype=jnp.int32)
    cidx = jnp.clip(col - kw // 2, 0, GRID_W - kw)[:, None] + jnp.arange(kw, dtype=jnp.int32)[None, :]
    rpb_cols = rpb[:, :, cidx - col[:, None] + (NA_COLS - 1)]
    L = ck.shape[1]

    def block(args):
        r, qr = args
        r0 = jnp.clip(r - kh // 2, 0, rows - kh)
        kr = lax.dynamic_slice_in_dim(kg, r0, kh, axis=1)
        vr = lax.dynamic_slice_in_dim(vg, r0, kh, axis=1)
        kn = kr[:, :, cidx]
        vn = vr[:, :, cidx]
        bias = rpb_cols[:, r0 + jnp.arange(kh, dtype=jnp.int32) - r + (NA_ROWS - 1)]
        s_loc = jnp.einsum('bqhd,biqjhd->bhqij', qr, kn).astype(jnp.float32) * ATTN_SCALE
        s_loc = s_loc + bias.transpose(0, 2, 1, 3)[None].astype(jnp.float32)
        s_loc = s_loc.reshape(B, H, GRID_W, kh * kw)
        s_ctx = jnp.einsum('bqhd,bshd->bhqs', qr, ck).astype(jnp.float32) * ATTN_SCALE
        p = jax.nn.softmax(jnp.concatenate([s_loc, s_ctx], axis=-1), axis=-1).astype(v.dtype)
        p_loc = p[..., :kh * kw].reshape(B, H, GRID_W, kh, kw)
        return (jnp.einsum('bhqij,biqjhd->bqhd', p_loc, vn)
                + jnp.einsum('bhqs,bshd->bqhd', p[..., kh * kw:kh * kw + L], cv))

    o = lax.map(block, (jnp.arange(rows, dtype=jnp.int32), qg))
    return o.transpose(1, 0, 2, 3, 4).reshape(B, S, H * DH)

def _merge(outs, gate_logits, w_branch, w_out):
    g = jax.nn.sigmoid(gate_logits.astype(jnp.float32)).astype(gate_logits.dtype)
    g = g.reshape(*g.shape[:-1], N_BRANCHES, D_MODEL)
    y = g[..., 0, :] * (outs[0] @ w_branch[0])
    for n in range(1, N_BRANCHES):
        y = y + g[..., n, :] * (outs[n] @ w_branch[n])
    return y @ w_out

def _route(hf, w_router, router_bias):
    scores = jax.nn.sigmoid((hf @ w_router).astype(jnp.float32))
    sel = scores + router_bias.astype(jnp.float32)
    grouped = sel.reshape(-1, N_GROUPS, EXPERTS_PER_GROUP)
    group_score = lax.top_k(grouped, TOP_K)[0].sum(-1)
    best = jnp.argmax(group_score, axis=-1)
    in_group = (jnp.arange(N_EXPERTS) // EXPERTS_PER_GROUP)[None, :] == best[:, None]
    _, idx = lax.top_k(jnp.where(in_group, sel, NEG_INF), TOP_K)
    w = jnp.take_along_axis(scores, idx, axis=-1)
    w = w / jnp.sum(w, axis=-1, keepdims=True)
    return jnp.sum(jax.nn.one_hot(idx, N_EXPERTS, dtype=jnp.float32) * w[..., None], axis=1)

def _moe(h, w_router, router_bias, w_gate, w_up, w_down):
    shp = h.shape
    hf = h.reshape(-1, shp[-1])
    combine = _route(hf, w_router, router_bias).astype(h.dtype)
    y = jnp.zeros_like(hf)
    for e in range(N_EXPERTS):
        a = jax.nn.silu(hf @ w_gate[e]) * (hf @ w_up[e])
        y = y + combine[:, e:e + 1] * (a @ w_down[e])
    return y.reshape(shp)

def setup_inputs(seed: int = 0) -> dict:
    key = jax.random.key(seed)
    ks = jax.random.split(key, 24)

    def nrm(k, shape, s):
        return jax.random.normal(k, shape, jnp.float32) * s

    return {
        'x': nrm(ks[0], (BATCH, SEQ, D_MODEL), 1.0),
        'c': nrm(ks[1], (BATCH, D_MODEL), 1.0),
        'ctx': nrm(ks[2], (BATCH, CTX_LEN, D_MODEL), 1.0),
        'c_ctx': nrm(ks[3], (D_MODEL,), 1.0),
        'w_mod': nrm(ks[4], (DEPTH, D_MODEL, 6 * D_MODEL), 0.5 * D_MODEL ** -0.5),
        'b_mod': nrm(ks[5], (DEPTH, 6 * D_MODEL), 0.02),
        'norm1': 1.0 + nrm(ks[6], (DEPTH, D_MODEL), 0.1),
        'norm2': 1.0 + nrm(ks[7], (DEPTH, D_MODEL), 0.1),
        'w_in': nrm(ks[8], (DEPTH, D_MODEL, IN_COLS), D_MODEL ** -0.5),
        'q_norm_a': 1.0 + nrm(ks[9], (DEPTH, HEAD_DIM), 0.1),
        'k_norm_a': 1.0 + nrm(ks[10], (DEPTH, HEAD_DIM), 0.1),
        'sink_b': nrm(ks[11], (DEPTH, N_HEADS_B), 1.0),
        'rpb_n': nrm(ks[12], (DEPTH, N_HEADS_N, 2 * NA_ROWS - 1, 2 * NA_COLS - 1), 0.5),
        'w_branch': nrm(ks[13], (DEPTH, N_BRANCHES, BRANCH_WIDTH, D_MODEL), BRANCH_WIDTH ** -0.5),
        'w_out': nrm(ks[14], (DEPTH, D_MODEL, D_MODEL), D_MODEL ** -0.5),
        'w_router': nrm(ks[15], (D_MODEL, N_EXPERTS), D_MODEL ** -0.5),
        'router_bias': nrm(ks[16], (N_EXPERTS,), 0.01),
        'w_e_gate': nrm(ks[17], (DEPTH, N_EXPERTS, D_MODEL, D_FF_EXPERT), D_MODEL ** -0.5),
        'w_e_up': nrm(ks[18], (DEPTH, N_EXPERTS, D_MODEL, D_FF_EXPERT), D_MODEL ** -0.5),
        'w_e_down': nrm(ks[19], (DEPTH, N_EXPERTS, D_FF_EXPERT, D_MODEL), D_FF_EXPERT ** -0.5),
        'final_norm': 1.0 + nrm(ks[20], (D_MODEL,), 0.1),
    }

def reference(x, c, ctx, c_ctx, w_mod, b_mod, norm1, norm2, w_in, q_norm_a, k_norm_a, sink_b,
              rpb_n, w_branch, w_out, w_router, router_bias, w_e_gate, w_e_up, w_e_down, final_norm):
    S = x.shape[1]
    rows = S // GRID_W
    cos, sin = _rope_tables(S)
    for l in range(DEPTH):
        last = l == DEPTH - 1
        mod = (jax.nn.silu(c) @ w_mod[l] + b_mod[l])[:, None, :]
        mod_c = (jax.nn.silu(c_ctx) @ w_mod[l] + b_mod[l])[None, None, :]
        sh1, sc1, g1, sh2, sc2, g2 = jnp.split(mod, 6, axis=-1)
        csh1, csc1, cg1, csh2, csc2, cg2 = jnp.split(mod_c, 6, axis=-1)

        h = _modulate(x, norm1[l], sh1, sc1)
        hc = _modulate(ctx, norm1[l], csh1, csc1)
        q_a, k_a, v_a, q_b, k_b, v_b, q_n, k_n, v_n, gate_l = jnp.split(h @ w_in[l], IN_OFFSETS, axis=-1)
        cq_a, ck_a, cv_a, cq_b, ck_b, cv_b, cq_n, ck_n, cv_n, gate_c = jnp.split(hc @ w_in[l], IN_OFFSETS, axis=-1)

        ck_a = _rmsnorm(_heads(ck_a, N_KV_A), k_norm_a[l])
        cv_a = _heads(cv_a, N_KV_A)
        ck_b = _heads(ck_b, N_KV_B)
        cv_b = _heads(cv_b, N_KV_B)
        ck_n = _heads(ck_n, N_HEADS_N)
        cv_n = _heads(cv_n, N_HEADS_N)

        qa = _rope_2d(_rmsnorm(_heads(q_a, N_HEADS_A), q_norm_a[l]), cos, sin)
        ka = _rope_2d(_rmsnorm(_heads(k_a, N_KV_A), k_norm_a[l]), cos, sin)
        o_a = _global_attention(qa, ka, _heads(v_a, N_KV_A), ck_a, cv_a)
        qb = _rope_2d(_heads(q_b, N_HEADS_B), cos, sin)
        kb = _rope_2d(_heads(k_b, N_KV_B), cos, sin)
        o_b = _window_attention(qb, kb, _heads(v_b, N_KV_B), ck_b, cv_b, sink_b[l])
        o_n = _neighbourhood_attention(_heads(q_n, N_HEADS_N), _heads(k_n, N_HEADS_N), _heads(v_n, N_HEADS_N),
                                       ck_n, cv_n, rpb_n[l], rows)
        x = x + g1 * _merge((o_a, o_b, o_n), gate_l, w_branch[l], w_out[l])

        if not last:
            oc_a = _ctx_attention(_rmsnorm(_heads(cq_a, N_HEADS_A), q_norm_a[l]), ck_a, cv_a)
            oc_b = _ctx_attention(_heads(cq_b, N_HEADS_B), ck_b, cv_b, sink_b[l])
            oc_n = _ctx_attention(_heads(cq_n, N_HEADS_N), ck_n, cv_n)
            ctx = ctx + cg1 * _merge((oc_a, oc_b, oc_n), gate_c, w_branch[l], w_out[l])
            ctx = ctx + cg2 * _moe(_modulate(ctx, norm2[l], csh2, csc2), w_router, router_bias,
                                   w_e_gate[l], w_e_up[l], w_e_down[l])

        x = x + g2 * _moe(_modulate(x, norm2[l], sh2, sc2), w_router, router_bias,
                          w_e_gate[l], w_e_up[l], w_e_down[l])
    return _rmsnorm(x, final_norm)


_drawn_inputs = setup_inputs


def setup_inputs(seed=0):
    import zlib

    import numpy as np

    out = dict(_drawn_inputs(seed))
    spreads = {}
    factors = {'q_norm_a': 5.666, 'k_norm_a': 3.109, 'sink_b': 8.0}
    for name, (base, spread) in spreads.items():
        noise = np.random.default_rng([zlib.crc32(name.encode()), seed]).standard_normal(out[name].shape)
        drawn = base * np.exp(spread * noise) if base else spread * noise
        out[name] = jnp.asarray(drawn.astype(out[name].dtype))
    for name, factor in factors.items():
        out[name] = (out[name] * factor).astype(out[name].dtype)
    return out
```

```python
from contextlib import ExitStack

import concourse.bass as bass
from concourse import mybir

F32 = mybir.dt.float32
F16 = mybir.dt.float16
BF16 = mybir.dt.bfloat16
I32 = mybir.dt.int32
ALU = mybir.AluOpType
ACT = mybir.ActivationFunctionType
AX = mybir.AxisListType.X

P = 128
D = 1024
KD = D // P
L = 2
SEQ, CTX = 256, 256
NT = (SEQ + CTX) // P
NLAT = SEQ // P
DH = 64
H = 8
NB = 3
BW = H * DH
GRID_W = 64
CW = 512
NE = 16
NBIAS = 4
LOOPS = (NE - 4) // 2
NG = 4
DFF = 512
CAP = P
PASS = NE * CAP
NMOD = 6 * D // CW
MODB_AT = 7
H1_ROWS = (13, 15, 17, 19)
SLOTS = 6
UNIT = KD * CW
EPS = 1e-6
NEG = -1e30
A, B, N = range(NB)
Q_COL = (0, 768, 1536)
KV_COL = (512, 1280)
KN_COL, VN_COL, GATE_COL = 2048, 2560, 3072

T_IDENT = 0
T_ROPEC = T_IDENT + P
T_ROPES = T_ROPEC + NLAT * DH
T_IOTA = T_ROPES + NLAT * DH
T_RANK = T_IOTA + P
T_EBASE = T_RANK + NE
T_COLS = T_EBASE + NE
M_BAND = 0
M_COLWIN = M_BAND + NLAT * CW
M_COLS = M_COLWIN + SEQ
H_PRE = 0
H_ONE = H_PRE + P
H_TOK = H_ONE + P
H_COLS = H_TOK + NT


def queries(l):
    return range(NT if l == 0 else NLAT)


def proj_units(l):
    nq = len(queries(l))
    return [("kvab", NT), ("qa", nq), ("qb", nq), ("kn", NT), ("vn", NT), ("qn", nq)]


def proj_jobs(l):
    return [(u, t) for u, n in proj_units(l) for t in range(n)]


def att_jobs(l):
    return [(b, t, h) for b in range(NB) for t in queries(l) for h in range(H)]


def biased(b, t):
    return b == B or (b == N and t < NLAT)


def merge_jobs(l):
    return [(n, half, t) for n in range(NB) for half in range(2) for t in queries(l)]


def before(jobs, l):
    return sum(len(jobs(x)) for x in range(l))


def out_jobs(l):
    return [(t, half) for t in queries(l) for half in range(2)]


def plan_units():
    order, landed, held = [], {}, {}
    total = [0] * SLOTS
    last = [None] * SLOTS

    def put(key, slot, dmas=1):
        order.append((key, slot, last[slot]))
        total[slot] += 16 * dmas
        landed[key] = (slot, total[slot])
        last[slot] = key

    for l in range(L):
        for j in range(NMOD):
            put(("mod", l, j), j % SLOTS)
    for l in range(L):
        names = [u for u, _ in proj_units(l)]
        names += [x for n in range(NB) for x in (f"wb{n}", f"g{n}0", f"g{n}1")] + ["wo0", "wo1"]
        for i, name in enumerate(names):
            put((name, l), i % SLOTS, 2 if name == "kvab" else 1)
        for s in range(SLOTS):
            held[l, s] = (last[s], total[s])
            total[s] += 16 * (NE // 2)
            last[s] = ("expert", l, s)
    return order, landed, held


def build(nc, t_in, out):
    x, c, ctx_in, c_ctx = t_in["x"], t_in["c"], t_in["ctx"], t_in["c_ctx"]
    order, landed, held = plan_units()
    mod_d = nc.dram_tensor("mod_d", [L, 2, 6 * D], F32, kind="Internal").ap()
    h2_d = [nc.dram_tensor(f"h2_d{l}", [len(queries(l)) * P, D], F32, kind="Internal").ap() for l in range(L)]
    y_d = [nc.dram_tensor(f"y_d{l}", [NT * NE * CAP, D], F32, kind="Internal").ap() for l in range(L)]

    with ExitStack() as es:
        def sb(name, shape, dt=F32):
            return es.enter_context(nc.sbuf_tensor(name + "_sb", shape, dt))

        def sem(name):
            return es.enter_context(nc.semaphore(name))

        ring = sb("ring", [P, SLOTS, KD, CW])
        X = sb("X", [P, NT, D])
        HT = sb("HT", [P, KD, NT * P])
        QR = sb("QR", [P, NB * 4 * NT * P])
        KR = sb("KR", [P, 6 * D])
        MB = sb("MB", [P, 4 * D])
        WK = sb("WK", [P, 2 * D])
        tab = sb("tab", [P, T_COLS])
        tabh = sb("tabh", [P, H_COLS], F16)
        masks = sb("masks", [P, M_COLS], BF16)
        wr = sb("wr", [P, KD, NE])
        gq = sb("gq", [P, 2, DH])
        sink = sb("sink", [P, L, H])
        rbias = sb("rbias", [P, NE])
        ssq = sb("ssq", [P, NT])
        rms = sb("rms", [P, NT])
        rstd = sb("rstd", [P, NT])
        hss = sb("hss", [P, H])
        hrt = sb("hrt", [P, H])
        hrs = sb("hrs", [P, H])
        cT = sb("cT", [P, KD, 2])
        mx = sb("mx", [P, 4])
        mx2 = sb("mx2", [P, 4])
        nmx = sb("nmx", [P, 4])
        psm = sb("psm", [P, 4])
        rcp = sb("rcp", [P, 4])
        r_m = sb("r_m", [P, NT])
        r_n = sb("r_n", [P, NT])
        r_w = sb("r_w", [P, NT, 2])
        posm = sb("posm", [P, NT, NE])
        selh = sb("selh", [P, NT, NE], F16)
        slot_i = sb("slot_i", [P, 2, NT], I32)
        idx_i = sb("idx_i", [P, NE], I32)
        sp_idx = sb("sp_idx", [P, 1], I32)
        sp_pad = sb("sp_pad", [P, 1])
        cnt = sb("cnt", [P, 1])
        flag = sb("flag", [P, 1], I32)
        bank = [es.enter_context(nc.psum_tensor(f"bank{i}", [P, CW], F32)) for i in range(8)]

        ident = tab[:, T_IDENT:T_IDENT + P]
        WR = [ring[:, s] for s in range(SLOTS)]
        wdown = [ring[:, s].rearrange("p a b -> p (a b)").rearrange("p (k n) -> p k n", k=4) for s in range(SLOTS)]
        qT = [QR[:, b * 4 * NT * P:(b + 1) * 4 * NT * P].rearrange("p (j n) -> p j n", j=4) for b in range(NB)]
        kT = [KR[:, 0:512].rearrange("p (j n) -> p j n", j=1), KR[:, 512:1024].rearrange("p (j n) -> p j n", j=1),
              KR[:, 1024:3072].rearrange("p (j n) -> p j n", j=4)]
        vAB = KR[:, 3072:4096].rearrange("p (t b n) -> p t b n", t=NT, b=2)
        vN = KR[:, 4096:6144].rearrange("p (t n) -> p t n", t=NT)
        Y = KR[:, 0:4096].rearrange("p (t n) -> p t n", t=NT)
        gout = KR[:, 4096:6144].rearrange("p (s n) -> p s n", s=2)
        modb = MB[:, :].rearrange("p (s a n) -> p s a n", s=2, a=2)
        r_sc, r_sel, r_key, r_o1, r_o2, r_pos = (
            MB[:, NT * NE * i:NT * NE * (i + 1)].rearrange("p (t e) -> p t e", t=NT) for i in range(6))
        r_pair = MB[:, 512:512 + NT * NG * 6].rearrange("p (g k) -> p g k", k=6)
        r_g, r_gk = (MB[:, 640 + NT * NG * i:640 + NT * NG * (i + 1)].rearrange("p (t g) -> p t g", t=NT)
                     for i in range(2))
        slotf = MB[:, 704:704 + 2 * NT].rearrange("p (t k) -> p t k", t=NT)
        nat = [MB[:, 512 * i:512 * i + 512] for i in range(2)]
        hn_a, rope1, rope2, hsq = (MB[:, 512 * i:512 * i + 512] for i in range(2, 6))
        sbank = [bank[0], bank[1], bank[2], bank[7]]
        bias = [MB[:, 3072 + SEQ * i:3072 + SEQ * i + SEQ] for i in range(NBIAS)]
        probs = [MB[:, 520 * i:520 * i + CW + 1] for i in range(4)]
        hn = [WK[:, D * i:D * i + D] for i in range(2)]
        S = [WK[:, 0:CW + 1], MB[:, 2080:2080 + CW + 1]]
        PT = [WK[:, 1024 + 512 * i:1536 + 512 * i].rearrange("p (k q) -> p k q", k=4) for i in range(2)]
        sg = [WK[:, 512 * i:512 * i + 512] for i in range(2)]
        wtmp = [WK[:, 1024 + 512 * i:1536 + 512 * i] for i in range(2)]
        junk = [[W[:, D * t:D * t + D] for t in range(NT)] for W in (MB, QR)]
        bmod = [QR[0:2, 0:6 * D], KR[0:2, 0:6 * D]]
        nrow = [HT[0:2, :, :].rearrange("p a b -> p (a b)")[:, 0:2 * D].rearrange("p (n m) -> p n m", n=2),
                QR[0:2, 2 * D:4 * D].rearrange("p (n m) -> p n m", n=2)]
        mrow = [[W[0:2, CW * i:CW * i + CW] for i in range(4)] for W in (WK, QR)]
        crow = X[0:2, 3, :]
        oneh = [QR[:, D * t:D * t + D].bitcast(F16) for t in range(NT)]
        hg = [QR[:, D * i:D * i + D] for i in range(2)]
        hgT = [QR[:, 2 * D + D * i:3 * D + D * i].rearrange("p (k n) -> p k n", k=KD) for i in range(2)]
        esg = QR[:, 4096:4608]
        ea = QR[:, 4608:5120]
        eaT = QR[:, 5120:5632].rearrange("p (k n) -> p k n", k=4)
        yd = [KR[:, D * i:D * i + D] for i in range(2)]
        sp_oh = KR[:, 2048:2048 + NT * 64].bitcast(F16).rearrange("p (t n) -> p t n", t=NT)
        HTf = HT[:, :, :].rearrange("p a b -> p (a b)")
        ygat = [[HTf[:, D * (2 * i + k):D * (2 * i + k) + D] for k in range(2)] for i in range(2)]

        w_in_slot = [sem(f"w_in_slot{s}") for s in range(SLOTS)]
        tab_in = sem("tab_in")
        const_in = sem("const_in")
        x_in = sem("x_in")
        c_in = sem("c_in")
        bmod_in = [sem(f"bmod_in{l}") for l in range(L)]
        gq_in = sem("gq_in")
        cT_mm = sem("cT_mm")
        cT_ready = sem("cT_ready")
        mod_mm = sem("mod_mm")
        mod_row = sem("mod_row")
        mod_store = [sem(f"mod_store{i}") for i in range(4)]
        modb_in = sem("modb_in")
        gout_in = sem("gout_in")
        sq_done = sem("sq_done")
        ms_done = sem("ms_done")
        rms_done = sem("rms_done")
        dve_step = sem("dve_step")
        hn_ready = sem("hn_ready")
        h_tr = sem("h_tr")
        h_copied = sem("h_copied")
        h2_store = [sem(f"h2_store{i}") for i in range(2)]
        proj_mm = sem("proj_mm")
        hsq_done = sem("hsq_done")
        hms_done = sem("hms_done")
        hrt_done = sem("hrt_done")
        v_used = sem("v_used")
        nat_ready = sem("nat_ready")
        nat_tr = sem("nat_tr")
        nat_copied = sem("nat_copied")
        qk_mm = sem("qk_mm")
        bias_in = [sem(f"bias_in{i}") for i in range(NBIAS)]
        bias_ready = sem("bias_ready")
        nm_ready = sem("nm_ready")
        exp_done = sem("exp_done")
        p_norm = sem("p_norm")
        pt_tr = sem("pt_tr")
        pt_copied = [sem(f"pt_copied{i}") for i in range(2)]
        pv_mm = sem("pv_mm")
        o_copied = sem("o_copied")
        gate_mm = sem("gate_mm")
        branch_mm = sem("branch_mm")
        sig_ready = sem("sig_ready")
        merged = sem("merged")
        y_tr = sem("y_tr")
        y_copied = sem("y_copied")
        out_mm = sem("out_mm")
        x_att = sem("x_att")
        router_mm = sem("router_mm")
        score_ready = sem("score_ready")
        sel_ready = sem("sel_ready")
        pos_mm = sem("pos_mm")
        oneh_ready = sem("oneh_ready")
        idx_mm = sem("idx_mm")
        idx_ready = sem("idx_ready")
        flag_ready = sem("flag_ready")
        hg_in = [sem(f"hg_in{i}") for i in range(2)]
        hg_tr = sem("hg_tr")
        hgT_copied = sem("hgT_copied")
        eg_mm = sem("eg_mm")
        eu_mm = sem("eu_mm")
        silu_done = sem("silu_done")
        ea_ready = sem("ea_ready")
        ea_tr = sem("ea_tr")
        eaT_copied = sem("eaT_copied")
        ed_mm = sem("ed_mm")
        yd_lo = sem("yd_lo")
        yd_hi = sem("yd_hi")
        y_out = [sem(f"y_out{i}") for i in range(2)]
        ygat_in = [sem(f"ygat_in{i}") for i in range(2)]
        x_moe = sem("x_moe")
        out_store = sem("out_store")
        sp = [{n: sem(f"sp{l}_{n}") for n in (
            "onehot", "idx_mm", "idx", "pad", "rows_in", "w_in", "hg_tr", "hgT", "up_mm", "silu", "a", "a_tr", "aT",
            "down_mm", "y", "stored", "step")} for l in range(L)]

        def releases(key):
            if key[0] == "mod":
                return mod_mm, NMOD * key[1] + key[2] + 1
            if key[0] == "expert":
                _, l, s = key
                done = (eg_mm, eu_mm, ed_mm)[s % 3]
                n = NE * l + NE - 1 + s // 3
                return done, n * (2 if s % 3 == 2 else 1)
            name, l = key
            if name in ("wo0", "wo1"):
                return out_mm, before(out_jobs, l) + len(out_jobs(l))
            if name.startswith("wb"):
                return branch_mm, before(merge_jobs, l) + (int(name[2]) + 1) * 2 * len(queries(l))
            if name.startswith("g"):
                n, half = int(name[1]), int(name[2])
                return gate_mm, before(merge_jobs, l) + (2 * n + half + 1) * len(queries(l))
            n = 0
            for u, tiles in proj_units(l):
                n += tiles
                if u == name:
                    return proj_mm, before(proj_jobs, l) + n

        block = es.enter_context(nc.Block())

        @block.sync
        def _(eng):
            def source(key):
                if key[0] == "mod":
                    return [(slice(0, CW), t_in["w_mod"][key[1], :, CW * key[2]:CW * key[2] + CW])]
                name, l = key
                w = t_in["w_in"][l]
                if name == "kvab":
                    return [(slice(256 * i, 256 * i + 256), w[:, KV_COL[i]:KV_COL[i] + 256]) for i in range(2)]
                col = {"qa": Q_COL[A], "qb": Q_COL[B], "qn": Q_COL[N], "kn": KN_COL, "vn": VN_COL}.get(name)
                if name in ("wo0", "wo1"):
                    w, col = t_in["w_out"][l], CW * int(name[2])
                elif col is None:
                    col = GATE_COL + D * int(name[1]) + CW * int(name[2])
                return [(slice(0, CW), w[:, col:col + CW])]

            def load(key, slot, prev):
                if prev is not None:
                    eng.wait_ge(*releases(prev))
                if key[0].startswith("wb"):
                    src = t_in["w_branch"][key[1], int(key[0][2])].rearrange("(k p) n -> p k n", p=P)
                    eng.dma_start(wdown[slot], src).then_inc(w_in_slot[slot], 16)
                    return
                for cols, src in source(key):
                    eng.dma_start(WR[slot][:, :, cols], src.rearrange("(k p) n -> p k n", p=P))\
                       .then_inc(w_in_slot[slot], 16)

            def expert_source(l, e, j):
                w = t_in[("w_e_gate", "w_e_up", "w_e_down")[j]]
                w = w[l, e] if isinstance(e, int) else w[l, bass.ds(e, 1)].rearrange("o k n -> (o k) n")
                return w.rearrange("(k p) n -> p k n", p=P)

            def load_expert(l, e, parity, j):
                slot = 3 * parity + j
                if isinstance(e, int) and e < 2:
                    eng.wait_ge(*releases(held[l, slot][0]))
                else:
                    n = NE * l + e - 1
                    eng.wait_ge((eg_mm, eu_mm, ed_mm)[j], n * (2 if j == 2 else 1))
                dst = wdown[slot] if j == 2 else WR[slot]
                eng.dma_start(dst, expert_source(l, e, j)).then_inc(w_in_slot[slot], 16)

            for key, slot, prev in order:
                if key[0] == "mod":
                    load(key, slot, prev)
            for l in range(L):
                for key, slot, prev in order:
                    if key[0] != "mod" and key[1] == l:
                        load(key, slot, prev)
                for e, j in ((0, 0), (0, 1), (1, 0), (1, 1), (0, 2), (2, 0), (2, 1), (1, 2)):
                    load_expert(l, e, e % 2, j)
                with eng.Fori(0, LOOPS) as i:
                    for o in (3, 4):
                        e = 2 * i + o
                        load_expert(l, e, o % 2, 0)
                        load_expert(l, e, o % 2, 1)
                        load_expert(l, e - 1, (o - 1) % 2, 2)
                for e, j in ((NE - 1, 0), (NE - 1, 1), (NE - 2, 2), (NE - 1, 2)):
                    load_expert(l, e, e % 2, j)

                eng.wait_ge(flag_ready, l + 1)
                most = eng.value_load(flag[0:1, 0:1], min_val=0, max_val=NT * P)
                with eng.If(most > CAP):
                    q = sp[l]
                    for i in range(2):
                        eng.wait_ge(y_out[i], 16 * (NE // 2) * (l + 1))
                    with eng.Fori(0, NT - 1) as r:
                        with eng.Fori(0, NE) as e:
                            n = r * NE + e
                            eng.wait_ge(q["onehot"], n + 1)
                            for j in range(3):
                                dst = wdown[2] if j == 2 else WR[j]
                                eng.dma_start(dst, expert_source(l, e, j)).then_inc(q["w_in"], 16)
                    eng.wait_ge(q["w_in"], 48 * NE * (NT - 1))
                    eng.wait_ge(q["stored"], 16 * NE * (NT - 1))

        @block.gpsimd
        def _(eng):
            dma = eng.dma_start
            def load_mod_rows(l):
                dma(bmod[l], t_in["b_mod"][l].unsqueeze(0).broadcast_to([2, 6 * D])).then_inc(bmod_in[l], 16)
                for i, name in enumerate(("norm1", "norm2")):
                    dma(nrow[l][:, i], t_in[name][l].unsqueeze(0).broadcast_to([2, D])).then_inc(bmod_in[l], 16)

            def load_modb(l, first):
                for s in range(2):
                    for a, part in ((0, first + 1), (1, first)):
                        dma(modb[:, s, a], mod_d[l, s, part * D:(part + 1) * D].unsqueeze(0).broadcast_to([P, D]))\
                            .then_inc(modb_in, 16)

            load_mod_rows(0)
            dma(masks[:, :], t_in["masks"]).then_inc(const_in, 16)
            dma(tabh[:, :], t_in["tabh"]).then_inc(const_in, 16)
            dma(sink[:, :, :], t_in["sink_b"].unsqueeze(0).broadcast_to([P, L, H])).then_inc(const_in, 16)
            dma(rbias[:, :], t_in["router_bias"].unsqueeze(0).broadcast_to([P, NE])).then_inc(const_in, 16)
            dma(wr[:, :, :], t_in["w_router"].rearrange("(k p) e -> p k e", p=P)).then_inc(const_in, 16)
            for i in range(L * NMOD):
                if i == NMOD:
                    eng.wait_ge(mod_row, NMOD)
                    load_mod_rows(1)
                eng.wait_ge(mod_row, i + 1)
                l, j = divmod(i, NMOD)
                dma(mod_d[l, :, CW * j:CW * j + CW], mrow[l][i % 4]).then_inc(mod_store[i % 4], 16)
                if i == MODB_AT:
                    for k in range(4):
                        eng.wait_ge(mod_store[k], 16)
                    eng.wait_ge(sq_done, NT)
                    load_modb(0, 0)
            for i in range(4):
                eng.wait_ge(mod_store[i], 16 * L * NMOD // 4)

            def load_gout(l, part):
                for s in range(2):
                    dma(gout[:, s], mod_d[l, s, part * D:(part + 1) * D].unsqueeze(0).broadcast_to([P, D]))\
                        .then_inc(gout_in, 16)

            for l in range(L):
                nq = len(queries(l))
                J0 = before(att_jobs, l)
                if l:
                    load_modb(l, 0)
                for i, name in enumerate(("q_norm_a", "k_norm_a")):
                    dma(gq[:, i], t_in[name][l].unsqueeze(0).broadcast_to([P, DH])).then_inc(gq_in, 16)
                if l == 0:
                    eng.wait_ge(const_in, 80)
                for n in range(NLAT * H):
                    i = n % NBIAS
                    eng.wait_ge(bias_in[i], 32 * ((l * NLAT * H + n) // NBIAS + 1))
                    eng.tensor_tensor(bias[i], bias[i], masks[:, M_COLWIN:M_COLWIN + SEQ],
                                      ALU.add).then_inc(bias_ready, 1)
                eng.wait_ge(pv_mm, J0 + len(att_jobs(l)))
                load_gout(l, 2)
                load_modb(l, 3)
                for t in range(nq):
                    eng.wait_ge(hn_ready, NT * (2 * l + 1) + t + 1)
                    dma(h2_d[l][P * t:P * t + P], hn[t % 2]).then_inc(h2_store[t % 2], 16)
                eng.wait_ge(x_att, before(out_jobs, l) + 2 * nq)
                load_gout(l, 5)
                for i in range(2):
                    eng.wait_ge(h2_store[i], 8 * (NT * l + nq))
                eng.wait_ge(idx_ready, l + 1)

                def gather(e):
                    n = NE * l + e
                    if n >= 2:
                        eng.wait_ge(hg_tr, n - 1)
                    eng.indirect_dma_start(hg[e % 2], None, h2_d[l],
                                           bass.IndirectOffsetOnAxis(ap=idx_i[:, e:e + 1], axis=0))\
                        .then_inc(hg_in[e % 2], 16)

                gather(0)
                gather(1)
                for e in range(NE):
                    if e + 2 < NE:
                        gather(e + 2)
                    eng.wait_ge(yd_lo, NE * l + e + 1)
                    eng.wait_ge(yd_hi, NE * l + e + 1)
                    dma(y_d[l][CAP * e:CAP * e + CAP], yd[e % 2]).then_inc(y_out[e % 2], 16)
                for i in range(2):
                    eng.wait_ge(y_out[i], 16 * (NE // 2) * (l + 1))

                def gather_outputs(table):
                    for t in range(nq):
                        if t >= 2:
                            eng.wait_ge(x_moe, NT * l + t - 1)
                        for k in range(2):
                            eng.indirect_dma_start(ygat[t % 2][k], None, table,
                                                   bass.IndirectOffsetOnAxis(ap=slot_i[:, k, t:t + 1], axis=0))\
                                .then_inc(ygat_in[t % 2], 16)

                eng.wait_ge(flag_ready, l + 1)
                most = eng.value_load(flag[0:1, 0:1], min_val=0, max_val=NT * P)
                with eng.If(most > CAP):
                    q = sp[l]
                    with eng.Fori(0, NT - 1) as r:
                        with eng.Fori(0, NE) as e:
                            n = r * NE + e
                            eng.wait_ge(q["idx"], n + 1)
                            eng.tensor_tensor(sp_pad[:, :], rbias[:, 0:1], rbias[:, 0:1], ALU.add).then_inc(q["pad"], 1)
                            eng.indirect_dma_start(hg[0], None, h2_d[l],
                                                   bass.IndirectOffsetOnAxis(ap=sp_idx[:, 0:1], axis=0))\
                                .then_inc(q["rows_in"], 16)
                            eng.wait_ge(q["pad"], n + 1)
                            eng.wait_ge(q["y"], n + 1)
                            row = r * PASS + e * CAP + PASS
                            dma(y_d[l][bass.ds(row, CAP)], yd[0]).then_inc(q["stored"], 16)
                            eng.wait_ge(q["stored"], 16 * (n + 1))

                    gather_outputs(y_d[l])
                with eng.If(most <= CAP):
                    gather_outputs(y_d[l][0:PASS])

            dma(modb[:, 0, 0], t_in["final_norm"].unsqueeze(0).broadcast_to([P, D])).then_inc(const_in, 16)
            for t in range(NLAT):
                eng.wait_ge(hn_ready, NT * 3 + NLAT + t + 1)
                dma(out[0, P * t:P * t + P], hn[t % 2]).then_inc(out_store, 16)
            eng.wait_ge(out_store, 16 * NLAT)

        @block.scalar
        def _(eng):
            act = eng.activation
            eng.dma_start(crow[0:1], c).then_inc(c_in, 16)
            eng.dma_start(crow[1:2], c_ctx.unsqueeze(0)).then_inc(c_in, 16)
            eng.dma_start(tab[:, :], t_in["tab"]).then_inc(tab_in, 16)
            for t in range(NLAT):
                eng.dma_start(X[:, t], x[0, P * t:P * t + P]).then_inc(x_in, 16)
            eng.wait_ge(cT_mm, 1)
            act(cT[:, :, :].rearrange("p k s -> p (k s)"), bank[7][:, 0:2 * KD], ACT.Silu).then_inc(cT_ready, 1)
            for t in range(NLAT):
                eng.dma_start(X[:, NLAT + t], ctx_in[0, P * t:P * t + P]).then_inc(x_in, 16)

            def norm_stats(group, tiles):
                for t in tiles:
                    act(junk[min(group, 1)][t], X[:, t], ACT.Square, accum_out=ssq[:, t:t + 1]).then_inc(sq_done, 1)
                eng.wait_ge(ms_done, group + 1)
                act(rms[:, 0:len(tiles)], rms[:, 0:len(tiles)], ACT.Sqrt).then_inc(rms_done, 1)

            def copy_h(n, t):
                eng.wait_ge(h_tr, n + 1)
                for g in range(2):
                    src = bank[4 + 2 * (t % 2) + g][:, :].rearrange("p (k q) -> p k q", k=4)
                    act(HT[:, 4 * g:4 * g + 4, P * t:P * t + P], src, ACT.Copy).then_inc(h_copied, 1)

            n_sq = 0
            n_nat = 0
            n_v = 0
            for l in range(L):
                nq = len(queries(l))
                if l == 0:
                    eng.wait_ge(x_in, 16 * NT)
                else:
                    eng.wait_ge(x_moe, NT)
                norm_stats(2 * l, range(NT))
                if l == 0:
                    eng.wait_ge(mod_row, NMOD)
                for t in range(NT):
                    copy_h(NT * 2 * l + t, t)
                if l == 0:
                    for i in range(4):
                        eng.wait_ge(mod_store[i], 16 * L * NMOD // 4)

                jobs = proj_jobs(l)
                late = []

                def copy_nat(u, t):
                    nonlocal n_nat
                    eng.wait_ge(nat_tr, n_nat + 1)
                    src = bank[4 + n_nat % 2][:, :].rearrange("p (j q) -> p j q", j=4)
                    cols = slice(P * t, P * t + P)
                    if u == "kvab":
                        dst = KR[:, 0:1024].rearrange("p (j n) -> p j n", j=2)[:, :, cols]
                        act(dst, src[:, 0:2], ACT.Copy).then_inc(nat_copied, 1)
                    else:
                        dst = kT[N] if u == "kn" else qT["abn".index(u[1])]
                        act(dst[:, :, cols], src, ACT.Copy).then_inc(nat_copied, 1)
                    n_nat += 1

                for j, (u, t) in enumerate(jobs):
                    n = before(proj_jobs, l) + j
                    pb = bank[j % 4]
                    if u in ("kvab", "qa"):
                        eng.wait_ge(proj_mm, n + 1)
                        if n_sq:
                            eng.wait_ge(hms_done, n_sq)
                        w = P if u == "kvab" else BW
                        act(hsq[:, 0:w], pb[:, 0:w], ACT.Square).then_inc(hsq_done, 1)
                        n_sq += 1
                    if u == "kvab":
                        v = pb[:, :].rearrange("p (b c n) -> p b c n", b=2, c=2)[:, :, 1]
                        act(vAB[:, t], v, ACT.Copy).then_inc(v_used, 1)
                        n_v += 1
                    if u == "vn":
                        eng.wait_ge(proj_mm, n + 1)
                        act(vN[:, t], pb[:, :], ACT.Copy).then_inc(v_used, 1)
                        n_v += 1
                    if u in ("kvab", "qa"):
                        eng.wait_ge(hms_done, n_sq)
                        k = 2 if u == "kvab" else H
                        act(hrt[:, 0:k], hss[:, 0:k], ACT.Sqrt).then_inc(hrt_done, 1)
                    late.append((u, t))
                    if len(late) > 2:
                        job = late.pop(0)
                        if job[0] != "vn":
                            copy_nat(*job)
                for job in late:
                    if job[0] != "vn":
                        copy_nat(*job)

                jobs = att_jobs(l)
                J0 = before(att_jobs, l)
                M = len(jobs)
                at_n = jobs.index((N, 0, 0))

                def load_bias(n):
                    t, h = divmod(n, H)
                    for half in range(2):
                        r = 2 * t + half
                        dst = bias[n % NBIAS][GRID_W * half:GRID_W * half + GRID_W].rearrange("c (i k) -> c i k", i=4)
                        eng.dma_start(dst, t_in["rpb"][l, h, 7 - r:11 - r].rearrange("i c k -> c i k"))\
                            .then_inc(bias_in[n % NBIAS], 16)

                for n in range(NBIAS):
                    load_bias(n)
                for s in range(M + 5):
                    n = s - at_n + NBIAS - 1
                    if NBIAS <= n < NLAT * H:
                        eng.wait_ge(nm_ready, J0 + s)
                        load_bias(n)
                    d = s - 3
                    if 0 <= d < M:
                        b, t, h = jobs[d]
                        ks = slice(0, NT) if t < NLAT else slice(NLAT, NT)
                        eng.wait_ge(pt_tr, J0 + d + 1)
                        if J0 + d >= 2:
                            eng.wait_ge(pv_mm, J0 + d - 1)
                        i = (J0 + d) % 2
                        act(PT[i][:, ks], bank[3 + i][:, :].rearrange("p (k q) -> p k q", k=4)[:, ks], ACT.Copy)\
                            .then_inc(pt_copied[i], 1)
                    if s < M:
                        a = J0 + s
                        b, t, h = jobs[s]
                        g = (J0 + s) // H
                        w = slice(0 if t < NLAT else SEQ, CW + 1 if b == B else CW)
                        eng.wait_ge(nm_ready, a + 1)
                        if s >= 4:
                            eng.wait_ge(pt_tr, a - 3)
                        src = S[a % 2] if biased(b, t) else sbank[a % 4]
                        act(probs[a % 4][:, w], src[:, w], ACT.Exp, bias=nmx[:, a % 4:a % 4 + 1],
                            accum_out=psm[:, a % 4:a % 4 + 1]).then_inc(exp_done, 1)
                    d = s - 5
                    if 0 <= d < M and jobs[d][2] == H - 1:
                        b, t, _ = jobs[d]
                        g = (J0 + d) // H
                        eng.wait_ge(pv_mm, J0 + d + 1)
                        act(qT[b][:, :, P * t:P * t + P], bank[5 + g % 2][:, :].rearrange("p (j q) -> p j q", j=4),
                            ACT.Copy).then_inc(o_copied, 1)

                for i, (n, half, t) in enumerate(merge_jobs(l)):
                    i += before(merge_jobs, l)
                    eng.wait_ge(gate_mm, i + 1)
                    if i >= 2:
                        eng.wait_ge(merged, i - 1)
                    act(sg[i % 2], bank[i % 2][:, :], ACT.Sigmoid).then_inc(sig_ready, 1)
                for t in range(nq):
                    eng.wait_ge(y_tr, (NT * l) + t + 1)
                    for g in range(2):
                        src = bank[4 + 2 * (t % 2) + g][:, :].rearrange("p (k q) -> p k q", k=4)
                        act(HT[:, 4 * g:4 * g + 4, P * t:P * t + P], src, ACT.Copy).then_inc(y_copied, 1)

                eng.wait_ge(x_att, before(out_jobs, l) + 2 * nq)
                norm_stats(2 * l + 1, range(nq))
                for t in range(nq):
                    copy_h(NT * (2 * l + 1) + t, t)
                eng.wait_ge(router_mm, l + 1)
                act(r_sc[:, 0:nq].rearrange("p t e -> p (t e)"), bank[0][:, 0:nq * NE], ACT.Sigmoid)\
                    .then_inc(score_ready, 1)

                def copy_hgT(n, parity):
                    eng.wait_ge(hg_tr, n + 1)
                    if not isinstance(n, int) or n >= 2:
                        eng.wait_ge(eu_mm, n - 1)
                    for g in range(2):
                        src = bank[6 + g][:, :].rearrange("p (k q) -> p k q", k=4)
                        act(hgT[parity][:, 4 * g:4 * g + 4], src, ACT.Copy).then_inc(hgT_copied, 1)

                def silu(n):
                    eng.wait_ge(eg_mm, n + 1)
                    eng.wait_ge(ea_ready, n)
                    act(esg, bank[0][:, :], ACT.Silu).then_inc(silu_done, 1)

                def store_hi(n, parity):
                    eng.wait_ge(ed_mm, 2 * n + 2)
                    if not isinstance(n, int) or n >= 2:
                        eng.wait_ge(y_out[parity], (n - parity) * 8)
                    act(yd[parity][:, CW:D], bank[5][:, :], ACT.Copy).then_inc(yd_hi, 1)

                E0 = NE * l
                def step(n, o):
                    silu(n)
                    store_hi(n - 1, (o - 1) % 2)
                    copy_hgT(n + 1, (o + 1) % 2)

                copy_hgT(E0, 0)
                silu(E0)
                copy_hgT(E0 + 1, 1)
                step(E0 + 1, 1)
                step(E0 + 2, 2)
                with eng.Fori(0, LOOPS) as i:
                    for o in (3, 4):
                        step(E0 + 2 * i + o, o)
                silu(E0 + NE - 1)
                store_hi(E0 + NE - 2, 0)
                store_hi(E0 + NE - 1, 1)

                eng.wait_ge(flag_ready, l + 1)
                most = eng.value_load(flag[0:1, 0:1], min_val=0, max_val=NT * P)
                with eng.If(most > CAP):
                    q = sp[l]
                    for i in range(2):
                        eng.wait_ge(y_out[i], 16 * (NE // 2) * (l + 1))
                    with eng.Fori(0, (NT - 1) * NE) as n:
                        eng.wait_ge(q["hg_tr"], n + 1)
                        for g in range(2):
                            src = bank[6 + g][:, :].rearrange("p (k q) -> p k q", k=4)
                            act(hgT[0][:, 4 * g:4 * g + 4], src, ACT.Copy).then_inc(q["hgT"], 1)
                        eng.wait_ge(q["up_mm"], n + 1)
                        act(esg, bank[0][:, :], ACT.Silu).then_inc(q["silu"], 1)

            eng.wait_ge(x_moe, NT + NLAT)
            norm_stats(4, range(NLAT))

        @block.vector
        def _(eng):
            tt, ts, stt = eng.tensor_tensor, eng.tensor_scalar, eng.scalar_tensor_tensor
            steps = [0]

            def link(ins):
                ins.then_inc(dve_step, 1)
                steps[0] += 1
                eng.wait_ge(dve_step, steps[0])


            def mod_rows(i):
                l, j = divmod(i, NMOD)
                if j == 0:
                    eng.wait_ge(bmod_in[l], 16 * 3)
                eng.wait_ge(mod_mm, i + 1)
                if i >= 4:
                    eng.wait_ge(mod_store[i % 4], 16 * (i // 4))
                row, b = mrow[l][i % 4], bmod[l][:, CW * j:CW * j + CW]
                part, half = divmod(j, 2)
                if part in (1, 4):
                    link(tt(row, bank[i % 4][0:2, :], b, ALU.add))
                    stt(row, row, 1.0, nrow[l][:, part // 4, CW * half:CW * half + CW], ALU.add, ALU.mult)\
                        .then_inc(mod_row, 1)
                else:
                    tt(row, bank[i % 4][0:2, :], b, ALU.add).then_inc(mod_row, 1)

            n_hn = 0

            def rms_rows(group, tiles, n_sq):
                eng.wait_ge(sq_done, n_sq)
                k = len(tiles)
                ts(rms[:, 0:k], ssq[:, 0:k], 1.0 / D, EPS, ALU.mult, ALU.add).then_inc(ms_done, 1)
                eng.wait_ge(rms_done, group + 1)
                link(eng.reciprocal(rstd[:, 0:k], rms[:, 0:k]))

            def modulated(tiles):
                nonlocal n_hn
                for t in tiles:
                    s = 0 if t < NLAT else 1
                    if n_hn >= 2:
                        eng.wait_ge(h_tr, n_hn - 1)
                    link(stt(hn[t % 2], X[:, t], rstd[:, t:t + 1], modb[:, s, 0], ALU.mult, ALU.mult))
                    tt(hn[t % 2], hn[t % 2], modb[:, s, 1], ALU.add).then_inc(hn_ready, 1)
                    n_hn += 1

            n_hsq, n_nat = 0, 0
            sq_total = NT
            rms_rows(0, range(NT), sq_total)
            for i in range(L * NMOD):
                mod_rows(i)
                if i in H1_ROWS:
                    t = H1_ROWS.index(i)
                    if t == 0:
                        for k in range(4):
                            eng.wait_ge(mod_store[k], 16 * NMOD // 4)
                        eng.wait_ge(modb_in, 64)
                    modulated([t])
            eng.wait_ge(tab_in, 16)
            eng.wait_ge(const_in, 80)
            for l in range(L):
                nq = len(queries(l))
                if l:
                    sq_total += NT
                    rms_rows(2 * l, range(NT), sq_total)
                    eng.wait_ge(modb_in, 64 * (2 * l + 1))
                    modulated(range(NT))

                eng.wait_ge(gq_in, 32 * (l + 1))

                def heads(v, k):
                    return v.rearrange("p (h d) -> p h d", h=k)

                def normed(pb, k, gain, scale_in_root):
                    nonlocal n_hsq
                    eng.wait_ge(hsq_done, n_hsq + 1)
                    link(eng.tensor_reduce(hss[:, 0:k], heads(hsq[:, 0:k * DH], k), AX, ALU.add))
                    if scale_in_root:
                        ts(hss[:, 0:k], hss[:, 0:k], DH * EPS, None, ALU.add).then_inc(hms_done, 1)
                    else:
                        ts(hss[:, 0:k], hss[:, 0:k], 1.0 / DH, EPS, ALU.mult, ALU.add).then_inc(hms_done, 1)
                    n_hsq += 1
                    eng.wait_ge(hrt_done, n_hsq)
                    link(eng.reciprocal(hrs[:, 0:k], hrt[:, 0:k]))
                    o = heads(hn_a[:, 0:k * DH], k)
                    link(tt(o, heads(pb, k), hrs[:, 0:k].unsqueeze(2).broadcast_to([P, k, DH]), ALU.mult))
                    return o, gq[:, gain].unsqueeze(1).broadcast_to([P, k, DH])

                def rotate(v, k, t, dst, view):
                    r1, r2 = rope1[:, 0:k * DH], rope2[:, 0:k * DH]
                    cos = tab[:, T_ROPEC + DH * t:T_ROPEC + DH * t + DH].unsqueeze(1).broadcast_to([P, k, DH])
                    tt(heads(r1, k), heads(v, k), cos, ALU.mult)
                    v5 = v.rearrange("p (h a x i) -> p h a x i", a=2, x=2, i=16)
                    o5 = r2.rearrange("p (h a x i) -> p h a x i", a=2, x=2, i=16)
                    for xx in range(2):
                        c0 = T_ROPES + DH * t + 32 * xx
                        sin = tab[:, c0:c0 + 32].rearrange("p (a i) -> p a i", a=2).unsqueeze(1)\
                            .broadcast_to([P, k, 2, 16])
                        ins = tt(o5[:, :, :, xx], v5[:, :, :, 1 - xx], sin, ALU.mult)
                    link(ins)
                    return tt(view(dst, False), view(r1, True), view(r2, True), ALU.add)

                def pair_view(v, source):
                    if source:
                        return v.rearrange("p (g j d) -> p g j d", g=2, j=4)
                    return v.rearrange("p (j g d) -> p g j d", g=2, j=4)

                def same_view(v, source):
                    return v

                for j, (u, t) in enumerate(proj_jobs(l)):
                    n = before(proj_jobs, l) + j
                    pb = bank[j % 4]
                    if u == "vn":
                        continue
                    eng.wait_ge(proj_mm, n + 1)
                    if n_nat >= 2:
                        eng.wait_ge(nat_tr, n_nat - 1)
                    dst = nat[n_nat % 2]
                    if u == "kvab":
                        o, gain = normed(pb[:, 0:P], 2, 1, False)
                        if t < NLAT:
                            link(tt(o, o, gain, ALU.mult))
                            link(rotate(hn_a[:, 0:P], 2, t, dst[:, 0:P], same_view))
                            link(eng.tensor_copy(hn_a[:, P:2 * P], pb[:, 2 * P:3 * P]))
                            last = rotate(hn_a[:, P:2 * P], 2, t, dst[:, P:2 * P], same_view)
                        else:
                            tt(heads(dst[:, 0:P], 2), o, gain, ALU.mult)
                            last = eng.tensor_copy(dst[:, P:2 * P], pb[:, 2 * P:3 * P])
                    elif u == "qa":
                        o, gain = normed(pb[:, :], H, 0, True)
                        if t < NLAT:
                            link(tt(o, o, gain, ALU.mult))
                            last = rotate(hn_a, H, t, dst, pair_view)
                        else:
                            link(tt(o, o, gain, ALU.mult))
                            last = eng.tensor_copy(pair_view(dst, False), pair_view(hn_a, True))
                    elif u == "qb":
                        if t < NLAT:
                            link(ts(hn_a, pb[:, :], DH ** -0.5, None, ALU.mult))
                            last = rotate(hn_a, H, t, dst, pair_view)
                        else:
                            last = ts(pair_view(dst, False), pair_view(pb[:, :], True), DH ** -0.5, None, ALU.mult)
                    elif u == "qn":
                        last = ts(dst, pb[:, :], DH ** -0.5, None, ALU.mult)
                    else:
                        last = eng.tensor_copy(dst, pb[:, :])
                    last.then_inc(nat_ready, 1)
                    n_nat += 1
                    eng.wait_ge(nat_ready, n_nat)

                jobs = att_jobs(l)
                J0 = before(att_jobs, l)
                M = len(jobs)
                n_bias = l * NLAT * H
                for s in range(M + 3):
                    if s < M:
                        a = J0 + s
                        b, t, h = jobs[s]
                        nm, bk = nmx[:, a % 4:a % 4 + 1], sbank[a % 4]
                        first = 0 if t < NLAT else SEQ
                        eng.wait_ge(qk_mm, a + 1)
                        if not biased(b, t):
                            eng.tensor_reduce(nm, bk[:, first:CW], AX, ALU.max, negate=True).then_inc(nm_ready, 1)
                        else:
                            if s >= 2:
                                eng.wait_ge(exp_done, a - 1)
                            dst, m1, m2 = S[a % 2], mx[:, a % 4:a % 4 + 1], mx2[:, a % 4:a % 4 + 1]
                            if b == B:
                                eng.tensor_copy(dst[:, CW:CW + 1], sink[:, l, h:h + 1])
                                k, add, start = slice(first, CW), M_BAND + CW * (t % NLAT), sink[:, l, h:h + 1]
                                add = masks[:, add + first:add + CW]
                            else:
                                n_bias += 1
                                link(eng.tensor_tensor_reduce(out=dst[:, SEQ:CW], in0=bk[:, SEQ:CW],
                                                              in1=masks[:, M_BAND + SEQ:M_BAND + CW], scale=1.0,
                                                              scalar=-3e38, op0=ALU.add, op1=ALU.max, accum_out=m2))
                                eng.wait_ge(bias_ready, n_bias)
                                k, add, start = slice(0, SEQ), bias[(n_bias - 1) % NBIAS], m2
                            link(eng.tensor_tensor_reduce(out=dst[:, k], in0=bk[:, k], in1=add, scale=1.0,
                                                          scalar=start, op0=ALU.add, op1=ALU.max, accum_out=m1))
                            ts(nm, m1, -1.0, None, ALU.mult).then_inc(nm_ready, 1)
                    d = s - 1
                    if 0 <= d < M:
                        a = J0 + d
                        b, t, h = jobs[d]
                        eng.wait_ge(exp_done, a + 1)
                        link(eng.reciprocal(rcp[:, a % 4:a % 4 + 1], psm[:, a % 4:a % 4 + 1]))
                        w = slice(0 if t < NLAT else SEQ, CW)
                        ts(probs[a % 4][:, w], probs[a % 4][:, w], rcp[:, a % 4:a % 4 + 1], None, ALU.mult)\
                            .then_inc(p_norm, 1)
                eng.wait_ge(pv_mm, J0 + M)

                for i, (n, half, t) in enumerate(merge_jobs(l)):
                    i += before(merge_jobs, l)
                    eng.wait_ge(sig_ready, i + 1)
                    eng.wait_ge(branch_mm, i + 1)
                    y = Y[:, t, CW * half:CW * half + CW]
                    if n == 0:
                        tt(y, sg[i % 2], bank[2 + i % 2][:, :], ALU.mult).then_inc(merged, 1)
                    else:
                        link(tt(wtmp[i % 2], sg[i % 2], bank[2 + i % 2][:, :], ALU.mult))
                        tt(y, y, wtmp[i % 2], ALU.add).then_inc(merged, 1)
                eng.wait_ge(merged, before(merge_jobs, l) + len(merge_jobs(l)))

                eng.wait_ge(gout_in, 32 * (2 * l + 1))
                for i, (t, half) in enumerate(out_jobs(l)):
                    n = before(out_jobs, l) + i
                    s = 0 if t < NLAT else 1
                    cols = slice(CW * half, CW * half + CW)
                    eng.wait_ge(out_mm, n + 1)
                    link(tt(wtmp[i % 2], bank[i % 4][:, :], gout[:, s, cols], ALU.mult))
                    tt(X[:, t, cols], X[:, t, cols], wtmp[i % 2], ALU.add).then_inc(x_att, 1)
                eng.wait_ge(x_att, before(out_jobs, l) + 2 * nq)

                sq_total += nq
                rms_rows(2 * l + 1, range(nq), sq_total)
                eng.wait_ge(modb_in, 64 * (2 * l + 2))
                for t in range(nq):
                    s = 0 if t < NLAT else 1
                    if n_hn >= 2:
                        eng.wait_ge(h_tr, n_hn - 1)
                    if t >= 2:
                        eng.wait_ge(h2_store[t % 2], 8 * NT * l + 16)
                    link(stt(hn[t % 2], X[:, t], rstd[:, t:t + 1], modb[:, s, 0], ALU.mult, ALU.mult))
                    tt(hn[t % 2], hn[t % 2], modb[:, s, 1], ALU.add).then_inc(hn_ready, 1)
                    n_hn += 1

                def bc(v, k):
                    return v.unsqueeze(2).broadcast_to([P, nq, k])

                R = [P, nq, NE]
                sc, sel, key, o1, o2, pos = (v[:, 0:nq] for v in (r_sc, r_sel, r_key, r_o1, r_o2, r_pos))
                rank = tab[:, T_RANK:T_RANK + NE].unsqueeze(1).broadcast_to(R)
                rank4 = tab[:, T_RANK:T_RANK + NG].unsqueeze(1).broadcast_to([P, nq, NG])
                eng.wait_ge(score_ready, l + 1)
                link(tt(sel, sc, rbias[:, :].unsqueeze(1).broadcast_to(R), ALU.add))
                g4 = sel.rearrange("p t (g e) -> p (t g) e", g=NG)
                pr = r_pair[:, 0:nq * NG]
                tt(pr[:, :, 0:3], g4[:, :, 0:3], g4[:, :, 1:4], ALU.add)
                tt(pr[:, :, 3:5], g4[:, :, 0:2], g4[:, :, 2:4], ALU.add)
                link(tt(pr[:, :, 5:6], g4[:, :, 0:1], g4[:, :, 3:4], ALU.add))
                gs, gk, m, m2 = r_g[:, 0:nq], r_gk[:, 0:nq], r_m[:, 0:nq], r_n[:, 0:nq]
                link(eng.tensor_reduce(gs.rearrange("p t g -> p (t g)"), pr, AX, ALU.max))
                link(eng.tensor_reduce(m, gs, AX, ALU.max))
                link(tt(gs, gs, bc(m, NG), ALU.is_equal))
                link(tt(gk, gs, rank4, ALU.mult))
                link(eng.tensor_reduce(m, gk, AX, ALU.max))
                link(tt(gs, gk, bc(m, NG), ALU.is_equal))
                link(ts(gk, gs, -1.0, -NEG, ALU.add, ALU.mult))

                def per_group(v):
                    return v.rearrange("p t g -> p (t g)").unsqueeze(2).broadcast_to([P, nq * NG, NG])

                link(tt(g4, g4, per_group(gs), ALU.mult))
                link(tt(g4, g4, per_group(gk), ALU.add))
                for k, o in enumerate((o1, o2)):
                    link(eng.tensor_reduce(m, sel, AX, ALU.max))
                    link(tt(o, sel, bc(m, NE), ALU.is_equal))
                    link(tt(key, o, rank, ALU.mult))
                    link(eng.tensor_reduce(m, key, AX, ALU.max))
                    link(tt(o, key, bc(m, NE), ALU.is_equal))
                    if k == 0:
                        link(stt(sel, o, 2 * NEG, sel, ALU.mult, ALU.add))
                link(tt(key, o1, o2, ALU.add))
                eng.tensor_copy(selh[:, 0:nq], key).then_inc(sel_ready, 1)
                for k, o in enumerate((o1, o2)):
                    link(tt(sel, sc, o, ALU.mult))
                    link(eng.tensor_reduce(r_w[:, 0:nq, k], sel, AX, ALU.add))
                link(tt(m, r_w[:, 0:nq, 0], r_w[:, 0:nq, 1], ALU.add))
                link(eng.reciprocal(m2, m))
                link(tt(r_w[:, 0:nq], r_w[:, 0:nq], bc(m2, 2), ALU.mult))
                eng.wait_ge(pos_mm, l + 1)
                link(eng.tensor_copy(pos.rearrange("p t e -> p (t e)"), bank[1][:, 0:nq * NE]))
                link(stt(posm[:, 0:nq], pos, 1.0, key, ALU.add, ALU.mult))
                link(ts(posm[:, 0:nq], posm[:, 0:nq], -1.0, None, ALU.add))
                iota = tab[:, T_IOTA:T_IOTA + P]
                for t in range(nq):
                    tt(oneh[t].rearrange("p (e j) -> p e j", e=NE), iota.unsqueeze(1).broadcast_to([P, NE, P]),
                       posm[:, t].unsqueeze(2).broadcast_to([P, NE, P]), ALU.is_equal).then_inc(oneh_ready, 1)
                ebase = tab[:, T_EBASE:T_EBASE + NE].unsqueeze(1).broadcast_to(R)
                link(ts(key, pos, float(CAP), None, ALU.is_ge))
                for r in range(2, NT):
                    link(stt(key, pos, float(CAP * r), key, ALU.is_ge, ALU.add))
                link(stt(pos, key, float(PASS - CAP), pos, ALU.mult, ALU.add))
                link(tt(pos, pos, ebase, ALU.add))
                for k, o in enumerate((o1, o2)):
                    link(tt(key, pos, o, ALU.mult))
                    link(eng.tensor_reduce(slotf[:, 0:nq, k], key, AX, ALU.add))
                    link(eng.tensor_copy(slot_i[:, k, 0:nq], slotf[:, 0:nq, k]))
                link(eng.tensor_reduce(cnt[:, :], bank[1][:, nq * NE:nq * NE + NE], AX, ALU.max))
                eng.tensor_copy(flag[:, :], cnt[:, :]).then_inc(flag_ready, 1)
                eng.wait_ge(idx_mm, l + 1)
                eng.tensor_copy(idx_i[:, :], bank[2][:, 0:NE]).then_inc(idx_ready, 1)

                def gated(n):
                    eng.wait_ge(silu_done, n + 1)
                    eng.wait_ge(eu_mm, n + 1)
                    eng.wait_ge(ea_tr, n)
                    tt(ea, esg, bank[1][:, :], ALU.mult).then_inc(ea_ready, 1)

                def store_lo(n, parity):
                    eng.wait_ge(ed_mm, 2 * n + 1)
                    if not isinstance(n, int) or n >= 2:
                        eng.wait_ge(y_out[parity], (n - parity) * 8)
                    eng.tensor_copy(yd[parity][:, 0:CW], bank[4][:, :]).then_inc(yd_lo, 1)

                def copy_eaT(n):
                    eng.wait_ge(ea_tr, n + 1)
                    eng.tensor_copy(eaT, bank[2][:, :].rearrange("p (k q) -> p k q", k=4)).then_inc(eaT_copied, 1)

                E0 = NE * l
                def step(n, o):
                    gated(n)
                    store_lo(n - 1, (o - 1) % 2)
                    copy_eaT(n)

                gated(E0)
                copy_eaT(E0)
                step(E0 + 1, 1)
                step(E0 + 2, 2)
                with eng.Fori(0, LOOPS) as i:
                    for o in (3, 4):
                        step(E0 + 2 * i + o, o)
                gated(E0 + NE - 1)
                store_lo(E0 + NE - 2, 0)
                copy_eaT(E0 + NE - 1)
                store_lo(E0 + NE - 1, 1)

                eng.wait_ge(flag_ready, l + 1)
                most = eng.value_load(flag[0:1, 0:1], min_val=0, max_val=NT * P)
                with eng.If(most > CAP):
                    q = sp[l]
                    for i in range(2):
                        eng.wait_ge(y_out[i], 16 * (NE // 2) * (l + 1))
                    with eng.Fori(0, NT - 1) as r:
                        ts(posm[:, 0:nq], posm[:, 0:nq], -float(CAP), None, ALU.add).then_inc(q["step"], 1)
                        with eng.Fori(0, NE) as e:
                            n = r * NE + e
                            eng.wait_ge(q["step"], r + 1)
                            for t in range(nq):
                                ins = ts(sp_oh[:, t], iota, posm[:, t, bass.ds(e, 1)], None, ALU.is_equal)
                            ins.then_inc(q["onehot"], 1)
                            eng.wait_ge(q["idx_mm"], n + 1)
                            eng.tensor_copy(sp_idx[:, :], bank[2][:, 0:1]).then_inc(q["idx"], 1)
                            eng.wait_ge(q["silu"], n + 1)
                            tt(ea, esg, bank[1][:, :], ALU.mult).then_inc(q["a"], 1)
                            eng.wait_ge(q["a_tr"], n + 1)
                            eng.tensor_copy(eaT, bank[3][:, :].rearrange("p (k q) -> p k q", k=4))\
                                .then_inc(q["aT"], 1)
                            eng.wait_ge(q["down_mm"], n + 1)
                            eng.tensor_copy(yd[0][:, 0:CW], bank[4][:, :])
                            eng.tensor_copy(yd[0][:, CW:D], bank[5][:, :]).then_inc(q["y"], 1)
                            eng.wait_ge(q["stored"], 16 * n + 16)

                eng.wait_ge(gout_in, 32 * (2 * l + 2))
                for t in range(nq):
                    s = 0 if t < NLAT else 1
                    g = NT * l + t
                    eng.wait_ge(ygat_in[t % 2], 32 * ((NT * l) // 2 + t // 2 + 1))
                    y0, y1 = ygat[t % 2]
                    link(ts(y0, y0, r_w[:, t, 0:1], None, ALU.mult))
                    link(stt(y0, y1, r_w[:, t, 1:2], y0, ALU.mult, ALU.add))
                    link(tt(y0, y0, gout[:, s], ALU.mult))
                    tt(X[:, t], X[:, t], y0, ALU.add).then_inc(x_moe, 1)
                eng.wait_ge(x_moe, NT * l + nq)

            rms_rows(4, range(NLAT), sq_total + NLAT)
            eng.wait_ge(const_in, 96)
            for t in range(NLAT):
                stt(hn[t], X[:, t], rstd[:, t:t + 1], modb[:, 0, 0], ALU.mult, ALU.mult).then_inc(hn_ready, 1)

        @block.tensor
        def _(eng):
            mm = eng.matmul

            def arrived(key):
                slot, n = landed[key]
                eng.wait_ge(w_in_slot[slot], n)
                return slot

            eng.wait_ge(c_in, 32)
            eng.wait_ge(tab_in, 16)
            for k in range(KD):
                ins = mm(bank[7][:, 2 * k:2 * k + 2], crow[:, P * k:P * k + P], tab[0:2, T_IDENT:T_IDENT + 2],
                         start=True, stop=True, is_transpose=True)
            ins.then_inc(cT_mm, 1)
            eng.wait_ge(cT_ready, 1)
            n_h = 0

            def transposes(src, dst, count):
                for k in range(count):
                    ins = mm(dst[:, P * k:P * k + P], src[:, P * k:P * k + P], ident,
                             start=True, stop=True, is_transpose=True)
                return ins

            def transpose_h(t):
                nonlocal n_h
                eng.wait_ge(hn_ready, n_h + 1)
                if n_h >= 2 and t >= 2:
                    eng.wait_ge(h_copied, 2 * (n_h - 1))
                for g in range(2):
                    ins = transposes(hn[t % 2][:, CW * g:CW * g + CW], bank[4 + 2 * (t % 2) + g], 4)
                ins.then_inc(h_tr, 1)
                n_h += 1

            for i in range(L * NMOD):
                l, j = divmod(i, NMOD)
                slot = arrived(("mod", l, j))
                if i >= 4:
                    eng.wait_ge(mod_row, i - 3)
                for k in range(KD):
                    ins = mm(bank[i % 4][0:2, :], cT[:, k, :], WR[slot][:, k], start=(k == 0), stop=(k == KD - 1))
                ins.then_inc(mod_mm, 1)
                if i - 2 in H1_ROWS:
                    transpose_h(H1_ROWS.index(i - 2))
            eng.wait_ge(mod_row, L * NMOD)

            n_nat, n_v, n_all_att = 0, 0, 0
            for l in range(L):
                nq = len(queries(l))
                if l:
                    eng.wait_ge(yd_lo, NE * l)
                    eng.wait_ge(yd_hi, NE * l)
                    for t in range(NT):
                        transpose_h(t)
                else:
                    eng.wait_ge(const_in, 80)
                eng.wait_ge(h_copied, 2 * n_h)

                jobs = proj_jobs(l)
                n_nat0, n_v0 = n_nat, n_v

                def transpose_nat(u):
                    nonlocal n_nat
                    eng.wait_ge(nat_ready, n_nat + 1)
                    if n_nat - n_nat0 >= 2:
                        eng.wait_ge(nat_copied, n_nat - 1)
                    transposes(nat[n_nat % 2], bank[4 + n_nat % 2], 2 if u == "kvab" else 4).then_inc(nat_tr, 1)
                    n_nat += 1

                for j, (u, t) in enumerate(jobs):
                    slot = arrived((u, l))
                    if j >= 4:
                        past = jobs[:j - 3]
                        nats = sum(x[0] != "vn" for x in past)
                        vs = sum(x[0] in ("vn", "kvab") for x in past)
                        eng.wait_ge(nat_ready, n_nat0 + nats)
                        eng.wait_ge(v_used, n_v0 + vs)
                    for k in range(KD):
                        ins = mm(bank[j % 4][:, :], HT[:, k, P * t:P * t + P], WR[slot][:, k],
                                 start=(k == 0), stop=(k == KD - 1))
                    ins.then_inc(proj_mm, 1)
                    if j >= 2 and jobs[j - 2][0] != "vn":
                        transpose_nat(jobs[j - 2][0])
                for u, _ in jobs[-2:]:
                    if u != "vn":
                        transpose_nat(u)
                n_v = n_v0 + 2 * NT
                eng.wait_ge(v_used, n_v)
                eng.wait_ge(nat_copied, n_nat)

                jobs = att_jobs(l)
                J0 = before(att_jobs, l)
                M = len(jobs)
                for s in range(M + 4):
                    if s < M:
                        a = J0 + s
                        b, t, h = jobs[s]
                        if s >= 4:
                            eng.wait_ge(exp_done, a - 3)
                        if b == N:
                            pair, side, kp = h // 2, h % 2, h // 2
                        else:
                            pair, side, kp = h % 4, h // 4, 0
                        part = slice(DH * side, DH * side + DH)
                        w = slice(0, CW) if t < NLAT else slice(SEQ, CW)
                        mm(sbank[a % 4][:, w], qT[b][part, pair, P * t:P * t + P], kT[b][part, kp, w],
                           start=True, stop=True).then_inc(qk_mm, 1)
                    d = s - 3
                    if 0 <= d < M:
                        a = J0 + d
                        b, t, h = jobs[d]
                        ks = range(0, NT) if t < NLAT else range(NLAT, NT)
                        eng.wait_ge(p_norm, a + 1)
                        if a >= 2:
                            eng.wait_ge(pt_copied[a % 2], a // 2)
                        for k in ks:
                            ins = mm(bank[3 + a % 2][:, P * k:P * k + P], probs[a % 4][:, P * k:P * k + P], ident,
                                     start=True, stop=True, is_transpose=True)
                        ins.then_inc(pt_tr, 1)
                    d = s - 4
                    if 0 <= d < M:
                        a = J0 + d
                        b, t, h = jobs[d]
                        g = a // H
                        ks = range(0, NT) if t < NLAT else range(NLAT, NT)
                        eng.wait_ge(pt_copied[a % 2], a // 2 + 1)
                        if h == 0 and g >= 2:
                            eng.wait_ge(o_copied, g - 1)
                        for k in ks:
                            v = vN[:, k, DH * h:DH * h + DH] if b == N else \
                                vAB[:, k, b, DH * (h // 4):DH * (h // 4) + DH]
                            dst = bank[5 + g % 2][DH * (h % 2):DH * (h % 2) + DH, P * (h // 2):P * (h // 2) + P]
                            ins = mm(dst, v, PT[a % 2][:, k], start=(k == ks[0]), stop=(k == NT - 1))
                        ins.then_inc(pv_mm, 1)
                eng.wait_ge(o_copied, (J0 + M) // H)

                for i, (n, half, t) in enumerate(merge_jobs(l)):
                    i += before(merge_jobs, l)
                    wb, wg = arrived((f"wb{n}", l)), arrived((f"g{n}{half}", l))
                    if i >= 2:
                        eng.wait_ge(merged, i - 1)
                    for k in range(KD):
                        ins = mm(bank[i % 2][:, :], HT[:, k, P * t:P * t + P], WR[wg][:, k],
                                 start=(k == 0), stop=(k == KD - 1))
                    ins.then_inc(gate_mm, 1)
                    for k in range(4):
                        ins = mm(bank[2 + i % 2][:, :], qT[n][:, k, P * t:P * t + P],
                                 wdown[wb][:, k, CW * half:CW * half + CW], start=(k == 0), stop=(k == 3))
                    ins.then_inc(branch_mm, 1)

                for t in range(nq):
                    eng.wait_ge(merged, before(merge_jobs, l) + len(merge_jobs(l)) - nq + t + 1)
                    if t >= 2:
                        eng.wait_ge(y_copied, 2 * (NT * l + t - 1))
                    for g in range(2):
                        ins = transposes(Y[:, t, CW * g:CW * g + CW], bank[4 + 2 * (t % 2) + g], 4)
                    ins.then_inc(y_tr, 1)
                for i, (t, half) in enumerate(out_jobs(l)):
                    slot = arrived((f"wo{half}", l))
                    eng.wait_ge(y_copied, 2 * (NT * l + t + 1))
                    if i >= 4:
                        eng.wait_ge(x_att, before(out_jobs, l) + i - 3)
                    for k in range(KD):
                        ins = mm(bank[i % 4][:, :], HT[:, k, P * t:P * t + P], WR[slot][:, k],
                                 start=(k == 0), stop=(k == KD - 1))
                    ins.then_inc(out_mm, 1)
                eng.wait_ge(y_copied, 2 * (NT * l + nq))

                for t in range(nq):
                    transpose_h(t)
                eng.wait_ge(h_copied, 2 * n_h)
                eng.wait_ge(x_att, before(out_jobs, l) + 2 * nq)
                for t in range(nq):
                    for k in range(KD):
                        ins = mm(bank[0][:, NE * t:NE * t + NE], HT[:, k, P * t:P * t + P], wr[:, k],
                                 start=(k == 0), stop=(k == KD - 1))
                ins.then_inc(router_mm, 1)
                eng.wait_ge(sel_ready, l + 1)
                ones = tabh[:, H_ONE:H_ONE + P]
                for t in range(nq):
                    for t2 in range(t + 1):
                        mm(bank[1][:, NE * t:NE * t + NE], ones if t2 < t else tabh[:, H_PRE:H_PRE + P],
                           selh[:, t2], start=(t2 == 0), stop=(t2 == t))
                for t in range(nq):
                    ins = mm(bank[1][:, NE * nq:NE * nq + NE], ones, selh[:, t], start=(t == 0), stop=(t == nq - 1))
                ins.then_inc(pos_mm, 1)
                eng.wait_ge(oneh_ready, NT * l + nq)
                for e in range(NE):
                    for t in range(nq):
                        ins = mm(bank[2][:, e:e + 1], oneh[t][:, P * e:P * e + P], tabh[:, H_TOK + t:H_TOK + t + 1],
                                 start=(t == 0), stop=(t == nq - 1))
                ins.then_inc(idx_mm, 1)

                base = {s: held[l, s][1] for s in range(SLOTS)}

                def transpose_rows(n, parity, k):
                    eng.wait_ge(hg_in[parity], k)
                    eng.wait_ge(hgT_copied, 2 * n)
                    for g in range(2):
                        ins = transposes(hg[parity][:, CW * g:CW * g + CW], bank[6 + g], 4)
                    ins.then_inc(hg_tr, 1)

                def up_gate(n, parity, k):
                    eng.wait_ge(hgT_copied, 2 * n + 2)
                    for j, (freed, done) in enumerate(((silu_done, eg_mm), (ea_ready, eu_mm))):
                        s = 3 * parity + j
                        eng.wait_ge(w_in_slot[s], base[s] + k)
                        eng.wait_ge(freed, n)
                        for c8 in range(KD):
                            ins = mm(bank[j][:, :], hgT[parity][:, c8], WR[s][:, c8], start=(c8 == 0),
                                     stop=(c8 == KD - 1))
                        ins.then_inc(done, 1)

                def down(n, parity, k):
                    s = 3 * parity + 2
                    eng.wait_ge(w_in_slot[s], base[s] + k)
                    eng.wait_ge(eaT_copied, n + 1)
                    for half, freed in enumerate((yd_lo, yd_hi)):
                        eng.wait_ge(freed, n)
                        for c4 in range(4):
                            ins = mm(bank[4 + half][:, :], eaT[:, c4], wdown[s][:, c4, CW * half:CW * half + CW],
                                     start=(c4 == 0), stop=(c4 == 3))
                        ins.then_inc(ed_mm, 1)

                def transpose_a(n):
                    eng.wait_ge(ea_ready, n + 1)
                    eng.wait_ge(eaT_copied, n)
                    transposes(ea, bank[2], 4).then_inc(ea_tr, 1)

                E0, G0 = NE * l, 16 * (NE // 2) * l
                eng.wait_ge(idx_ready, l + 1)
                transpose_rows(E0, 0, G0 + 16)
                up_gate(E0, 0, 16)
                transpose_a(E0)
                transpose_rows(E0 + 1, 1, G0 + 16)
                def step(n, o, before16):
                    up_gate(n, o % 2, before16 + 16)
                    even = 16 * (1 - o % 2)
                    down(n - 1, (o - 1) % 2, before16 + 16 - even)
                    transpose_a(n)
                    transpose_rows(n + 1, (o + 1) % 2, G0 + before16 + 32 - even)

                step(E0 + 1, 1, 0)
                step(E0 + 2, 2, 16)
                with eng.Fori(0, LOOPS) as i:
                    for o in (3, 4):
                        step(E0 + 2 * i + o, o, 16 * i + 16 * (o // 2))
                up_gate(E0 + NE - 1, 1, 8 * NE)
                down(E0 + NE - 2, 0, 8 * NE)
                transpose_a(E0 + NE - 1)
                down(E0 + NE - 1, 1, 8 * NE)

                eng.wait_ge(flag_ready, l + 1)
                most = eng.value_load(flag[0:1, 0:1], min_val=0, max_val=NT * P)
                with eng.If(most > CAP):
                    q = sp[l]
                    for i in range(2):
                        eng.wait_ge(y_out[i], 16 * (NE // 2) * (l + 1))
                    with eng.Fori(0, (NT - 1) * NE) as n:
                        eng.wait_ge(q["onehot"], n + 1)
                        for t in range(nq):
                            ins = mm(bank[2][:, 0:1], sp_oh[:, t], tabh[:, H_TOK + t:H_TOK + t + 1],
                                     start=(t == 0), stop=(t == nq - 1))
                        ins.then_inc(q["idx_mm"], 1)
                        eng.wait_ge(q["rows_in"], 16 * n + 16)
                        for g in range(2):
                            ins = transposes(hg[0][:, CW * g:CW * g + CW], bank[6 + g], 4)
                        ins.then_inc(q["hg_tr"], 1)
                        eng.wait_ge(q["hgT"], 2 * n + 2)
                        eng.wait_ge(q["w_in"], 48 * n + 48)
                        for j in range(2):
                            for k in range(KD):
                                ins = mm(bank[j][:, :], hgT[0][:, k], WR[j][:, k], start=(k == 0), stop=(k == KD - 1))
                        ins.then_inc(q["up_mm"], 1)
                        eng.wait_ge(q["a"], n + 1)
                        transposes(ea, bank[3], 4).then_inc(q["a_tr"], 1)
                        eng.wait_ge(q["aT"], n + 1)
                        for half in range(2):
                            for k in range(4):
                                ins = mm(bank[4 + half][:, :], eaT[:, k], wdown[2][:, k, CW * half:CW * half + CW],
                                         start=(k == 0), stop=(k == 3))
                        ins.then_inc(q["down_mm"], 1)


def tables():
    import numpy as np
    tab = np.zeros((P, T_COLS), np.float32)
    masks = np.zeros((P, M_COLS), mybir.dt.np(BF16))
    tab[:, T_IDENT:T_IDENT + P] = np.eye(P)
    tok = np.arange(SEQ)
    half = DH // 2
    inv = (np.float32(10000.0) ** (-np.arange(0, half, 2, dtype=np.float32) / np.float32(half))).astype(np.float32)
    ang = np.stack([(tok // GRID_W).astype(np.float32)[:, None] * inv,
                    (tok % GRID_W).astype(np.float32)[:, None] * inv], axis=1).astype(np.float32)
    cos, sin = np.cos(ang), np.sin(ang)
    for t in range(NLAT):
        rows = slice(P * t, P * t + P)
        tab[:, T_ROPEC + DH * t:T_ROPEC + DH * t + DH] = np.stack([cos[rows]] * 2, axis=2).reshape(P, DH)
        tab[:, T_ROPES + DH * t:T_ROPES + DH * t + DH] = np.stack([-sin[rows], sin[rows]], axis=1).reshape(P, DH)
        off = np.abs(tok[None, :] - tok[rows][:, None]) > 128
        masks[:, M_BAND + CW * t:M_BAND + CW * t + SEQ][off] = NEG
    c = np.arange(P) % GRID_W
    lo = np.clip(c - 8, 0, GRID_W - 16)[:, None]
    k = np.arange(GRID_W)[None, :]
    win = np.where((k >= lo) & (k < lo + 16), 0.0, NEG)
    masks[:, M_COLWIN:M_COLWIN + SEQ] = np.tile(win, (1, 4))
    tab[:, T_IOTA:T_IOTA + P] = np.arange(P)
    tab[:, T_RANK:T_RANK + NE] = NE - np.arange(NE)
    tab[:, T_EBASE:T_EBASE + NE] = CAP * np.arange(NE)
    tabh = np.zeros((P, H_COLS), np.float16)
    tabh[:, H_PRE:H_PRE + P] = np.arange(P)[:, None] < np.arange(P)[None, :]
    tabh[:, H_ONE:H_ONE + P] = 1
    tabh[:, H_TOK:H_TOK + NT] = np.arange(P)[:, None] + P * np.arange(NT)[None, :]
    return tab, masks, tabh


def kernel(**inputs):
    import numpy as np
    import concourse.bacc as bacc
    from concourse.bass_utils import run_bass_kernel_spmd as run

    arrays = {k: np.ascontiguousarray(v) for k, v in inputs.items() if k != "rpb_n"}
    padded = np.pad(np.asarray(inputs["rpb_n"]), ((0, 0), (0, 0), (0, 0), (48, 48)))
    arrays["rpb"] = np.ascontiguousarray(
        np.lib.stride_tricks.sliding_window_view(padded, GRID_W, axis=-1)[..., ::-1, :])
    arrays["tab"], arrays["masks"], arrays["tabh"] = tables()
    nc = bacc.Bacc("TRN2", target_bir_lowering=False, num_devices=1)
    t_in = {k: nc.dram_tensor(k, v.shape, mybir.dt.from_np(v.dtype), kind="ExternalInput").ap()
            for k, v in arrays.items()}
    out = nc.dram_tensor("out", (1, SEQ, D), F32, kind="ExternalOutput").ap()
    build(nc, t_in, out)
    return run(nc, [arrays], core_ids=[0]).results[0]["out"]
```

```python
from contextlib import ExitStack

import concourse.bass as bass
from concourse import mybir

F32 = mybir.dt.float32
F16 = mybir.dt.float16
BF16 = mybir.dt.bfloat16
I32 = mybir.dt.int32
ALU = mybir.AluOpType
ACT = mybir.ActivationFunctionType
AX = mybir.AxisListType.X

P = 128
D = 1024
KD = D // P
L = 2
SEQ, CTX = 256, 256
NT = (SEQ + CTX) // P
NLAT = SEQ // P
DH = 64
H = 8
NB = 3
BW = H * DH
GRID_W = 64
CW = 512
NE = 16
NBIAS = 4
LOOPS = (NE - 4) // 2
NG = 4
DFF = 512
CAP = P
PASS = NE * CAP
NMOD = 6 * D // CW
RING = (0, 1, 3, 4, 2, 5)
AHEAD = 3
H1_ROWS = (6, 7, 8, 9)
MOD_GAP = 8
MOD_BANK = (0, 1, 2, 3, 0, 1, 2, 3, 0, 1, 2, 3, 0, 4, 5, 0, 4, 5, 3, 4, 0, 1, 2, 3)
SLOTS = 6
UNIT = KD * CW
EPS = 1e-6
NEG = -1e30
A, B, N = range(NB)
Q_COL = (0, 768, 1536)
KV_COL = (512, 1280)
KN_COL, VN_COL, GATE_COL = 2048, 2560, 3072

T_IDENT = 0
T_ROPEC = T_IDENT + P
T_ROPES = T_ROPEC + NLAT * DH
T_IOTA = T_ROPES + NLAT * DH
T_RANK = T_IOTA + P
T_EBASE = T_RANK + NE
T_EPS = T_EBASE + NE
T_COLS = T_EPS + 1
M_BAND = 0
M_COLWIN = M_BAND + NLAT * CW
M_COLS = M_COLWIN + SEQ
H_PRE = 0
H_ONE = H_PRE + P
H_TOK = H_ONE + P
H_COLS = H_TOK + NT


def queries(l):
    return range(NT if l == 0 else NLAT)


def proj_units(l):
    nq = len(queries(l))
    return [("kvab", NT), ("qa", nq), ("qb", nq), ("kn", NT), ("vn", NT), ("qn", nq)]


def proj_jobs(l):
    return [(u, t) for u, n in proj_units(l) for t in range(n)]


def att_jobs(l):
    return [(b, t, h) for b in range(NB) for t in queries(l) for h in range(H)]


def biased(b, t):
    return b == B or (b == N and t < NLAT)


def merge_jobs(l):
    return [(n, half, t) for n in range(NB) for half in range(2) for t in queries(l)]


def before(jobs, l):
    return sum(len(jobs(x)) for x in range(l))


def out_jobs(l):
    return [(t, half) for t in queries(l) for half in range(2)]


def plan_units():
    sections, landed, held = [], {}, {}
    total = [0] * SLOTS
    last = [None] * SLOTS

    def put(key, slot, dmas):
        order.append((key, slot, last[slot]))
        total[slot] += 16 * dmas
        landed[key] = (slot, total[slot])
        last[slot] = key

    for l in range(L):
        order = []
        names = [("mod", l, j) for j in range(MOD_GAP * l, NMOD)]
        names += [(u, l) for u, _ in proj_units(l)]
        names += [(x, l) for n in range(NB) for x in (f"wb{n}", f"g{n}0", f"g{n}1")] + [("wo0", l), ("wo1", l)]
        if l == 0:
            names += [("mod", 1, j) for j in range(MOD_GAP)]
        first = SLOTS - len(names) % SLOTS if l == 0 else 0
        for i, name in enumerate(names):
            put(name, RING[(first + i) % SLOTS], 2 if name[0] == "kvab" else 1)
        sections.append(order)
        for s in range(SLOTS):
            held[l, s] = (last[s], total[s])
            total[s] += 16 * (NE // 2)
            last[s] = ("expert", l, s)
    return sections, landed, held


def build(nc, t_in, out):
    x, c, ctx_in, c_ctx = t_in["x"], t_in["c"], t_in["ctx"], t_in["c_ctx"]
    sections, landed, held = plan_units()
    mod_d = nc.dram_tensor("mod_d", [L, 2, 6 * D], F32, kind="Internal").ap()
    h2_d = [nc.dram_tensor(f"h2_d{l}", [len(queries(l)) * P, D], F32, kind="Internal").ap() for l in range(L)]
    y_d = [nc.dram_tensor(f"y_d{l}", [NT * NE * CAP, D], F32, kind="Internal").ap() for l in range(L)]

    with ExitStack() as es:
        def sb(name, shape, dt=F32):
            return es.enter_context(nc.sbuf_tensor(name + "_sb", shape, dt))

        def sem(name):
            return es.enter_context(nc.semaphore(name))

        ring = sb("ring", [P, SLOTS, KD, CW])
        X = sb("X", [P, NT, D])
        HT = sb("HT", [P, KD, NT * P])
        QR = sb("QR", [P, NB * 4 * NT * P])
        KR = sb("KR", [P, 6 * D])
        MB = sb("MB", [P, 4 * D])
        WK = sb("WK", [P, 2 * D])
        tab = sb("tab", [P, T_COLS])
        tabh = sb("tabh", [P, H_COLS], F16)
        masks = sb("masks", [P, M_COLS], BF16)
        wr = sb("wr", [P, KD, NE])
        gq = sb("gq", [P, 2, DH])
        sink = sb("sink", [P, L, H])
        rbias = sb("rbias", [P, NE])
        ssq = sb("ssq", [P, NT])
        rms = sb("rms", [P, NT])
        rstd = sb("rstd", [P, NT])
        hss = sb("hss", [P, H])
        hrt = sb("hrt", [P, H])
        hrs = sb("hrs", [P, H])
        cT = sb("cT", [P, KD, 2])
        mx = sb("mx", [P, 4])
        mx2 = sb("mx2", [P, 4])
        nmx = sb("nmx", [P, 4])
        psm = sb("psm", [P, 4])
        rcp = sb("rcp", [P, 4])
        r_m = sb("r_m", [P, NT])
        r_n = sb("r_n", [P, NT])
        r_w = sb("r_w", [P, NT, 2])
        posm = sb("posm", [P, NT, NE])
        selh = sb("selh", [P, NT, NE], F16)
        slot_i = sb("slot_i", [P, 2, NT], I32)
        idx_i = sb("idx_i", [P, NE], I32)
        sp_idx = sb("sp_idx", [P, 1], I32)
        sp_pad = sb("sp_pad", [P, 1])
        cnt = sb("cnt", [P, 1])
        flag = sb("flag", [P, 1], I32)
        bank = [es.enter_context(nc.psum_tensor(f"bank{i}", [P, CW], F32)) for i in range(8)]

        ident = tab[:, T_IDENT:T_IDENT + P]
        WR = [ring[:, s] for s in range(SLOTS)]
        wdown = [ring[:, s].rearrange("p a b -> p (a b)").rearrange("p (k n) -> p k n", k=4) for s in range(SLOTS)]
        qT = [QR[:, b * 4 * NT * P:(b + 1) * 4 * NT * P].rearrange("p (j n) -> p j n", j=4) for b in range(NB)]
        kT = [KR[:, 0:512].rearrange("p (j n) -> p j n", j=1), KR[:, 512:1024].rearrange("p (j n) -> p j n", j=1),
              KR[:, 1024:3072].rearrange("p (j n) -> p j n", j=4)]
        vAB = KR[:, 3072:4096].rearrange("p (t b n) -> p t b n", t=NT, b=2)
        vN = KR[:, 4096:6144].rearrange("p (t n) -> p t n", t=NT)
        Y = KR[:, 0:4096].rearrange("p (t n) -> p t n", t=NT)
        gout = KR[:, 4096:6144].rearrange("p (s n) -> p s n", s=2)
        modb = MB[:, :].rearrange("p (s a n) -> p s a n", s=2, a=2)
        r_sc, r_sel, r_key, r_o1, r_o2, r_pos = (
            MB[:, NT * NE * i:NT * NE * (i + 1)].rearrange("p (t e) -> p t e", t=NT) for i in range(6))
        r_pair = MB[:, 512:512 + NT * NG * 6].rearrange("p (g k) -> p g k", k=6)
        r_g, r_gk = (MB[:, 640 + NT * NG * i:640 + NT * NG * (i + 1)].rearrange("p (t g) -> p t g", t=NT)
                     for i in range(2))
        slotf = MB[:, 704:704 + 2 * NT].rearrange("p (t k) -> p t k", t=NT)
        nat = [MB[:, 512 * i:512 * i + 512] for i in range(2)]
        hn_a, rope1, rope2, hsq = (MB[:, 512 * i:512 * i + 512] for i in range(2, 6))
        sbank = [bank[0], bank[1], bank[2], bank[7]]
        bias = [MB[:, 3072 + SEQ * i:3072 + SEQ * i + SEQ] for i in range(NBIAS)]
        probs = [MB[:, 520 * i:520 * i + CW + 1] for i in range(4)]
        hn = [WK[:, D * i:D * i + D] for i in range(2)]
        S = [WK[:, 0:CW + 1], MB[:, 2080:2080 + CW + 1]]
        PT = [WK[:, 1024 + 512 * i:1536 + 512 * i].rearrange("p (k q) -> p k q", k=4) for i in range(2)]
        sg = [WK[:, 512 * i:512 * i + 512] for i in range(2)]
        wtmp = [WK[:, 1024 + 512 * i:1536 + 512 * i] for i in range(2)]
        junk = [[MB[:, D * t:D * t + D] for t in range(NT)], [QR[:, D * t:D * t + D] for t in range(NT)],
                [QR[:, 4 * D:5 * D], QR[:, 5 * D:6 * D], KR[:, 0:D], KR[:, D:2 * D]]]
        bmod = [QR[0:2, CW * j:CW * j + CW] for j in range(NMOD)] +\
               [QR[0:2, 4 * D + CW * j:4 * D + CW * j + CW] for j in range(4)] +\
               [KR[0:2, CW * j:CW * j + CW] for j in range(4)] + [WK[0:2, CW * j:CW * j + CW] for j in range(4)]
        nrow = [[KR[0:2, 2 * D:3 * D], KR[0:2, 0:D]], [KR[0:2, 2 * D:3 * D]] * 2]
        mrow = [KR[0:2, c0:c0 + CW] for c0 in (3 * D, 3 * D + CW, D, D + CW)]
        crow = X[0:2, 3, :]
        oneh = [QR[:, D * t:D * t + D].bitcast(F16) for t in range(NT)]
        hg = [QR[:, D * i:D * i + D] for i in range(2)]
        hgT = [QR[:, 2 * D + D * i:3 * D + D * i].rearrange("p (k n) -> p k n", k=KD) for i in range(2)]
        esg = QR[:, 4096:4608]
        ea = QR[:, 4608:5120]
        eaT = QR[:, 5120:5632].rearrange("p (k n) -> p k n", k=4)
        yd = [KR[:, D * i:D * i + D] for i in range(2)]
        sp_oh = QR[:, 5632:5632 + NT * 64].bitcast(F16).rearrange("p (t n) -> p t n", t=NT)
        HTf = HT[:, :, :].rearrange("p a b -> p (a b)")
        ygat = [[W[:, D * (2 * i + k):D * (2 * i + k) + D] for k in range(2)] for W in (HTf, QR) for i in range(2)]

        w_in_slot = [sem(f"w_in_slot{s}") for s in range(SLOTS)]
        tab_in = sem("tab_in")
        const_in = sem("const_in")
        x_in = sem("x_in")
        c_in = sem("c_in")
        bmod_in = [sem(f"bmod_in{l}") for l in range(L)]
        gq_in = sem("gq_in")
        cT_mm = sem("cT_mm")
        cT_ready = sem("cT_ready")
        mod_mm = sem("mod_mm")
        mod_row = sem("mod_row")
        mod_store = [sem(f"mod_store{i}") for i in range(4)]
        modb_in = sem("modb_in")
        gout_in = sem("gout_in")
        sq_done = sem("sq_done")
        rms_done = sem("rms_done")
        dve_step = sem("dve_step")
        hn_ready = sem("hn_ready")
        h_tr = sem("h_tr")
        h_copied = sem("h_copied")
        h2_store = [sem(f"h2_store{i}") for i in range(2)]
        proj_mm = sem("proj_mm")
        hsq_done = sem("hsq_done")
        hms_done = sem("hms_done")
        hrt_done = sem("hrt_done")
        v_used = sem("v_used")
        nat_ready = sem("nat_ready")
        nat_tr = sem("nat_tr")
        nat_copied = sem("nat_copied")
        qk_mm = sem("qk_mm")
        bias_in = [sem(f"bias_in{i}") for i in range(NBIAS)]
        bias_ready = sem("bias_ready")
        nm_ready = sem("nm_ready")
        exp_done = sem("exp_done")
        p_norm = sem("p_norm")
        pt_tr = sem("pt_tr")
        pt_copied = [sem(f"pt_copied{i}") for i in range(2)]
        pv_mm = sem("pv_mm")
        o_copied = sem("o_copied")
        gate_mm = sem("gate_mm")
        branch_mm = sem("branch_mm")
        sig_ready = sem("sig_ready")
        merged = sem("merged")
        y_tr = sem("y_tr")
        y_copied = sem("y_copied")
        out_mm = sem("out_mm")
        x_att = sem("x_att")
        router_mm = sem("router_mm")
        score_ready = sem("score_ready")
        sel_ready = sem("sel_ready")
        pos_mm = sem("pos_mm")
        oneh_ready = sem("oneh_ready")
        idx_mm = sem("idx_mm")
        idx_ready = sem("idx_ready")
        flag_ready = sem("flag_ready")
        hg_in = [sem(f"hg_in{i}") for i in range(2)]
        hg_tr = sem("hg_tr")
        hgT_copied = sem("hgT_copied")
        eg_mm = sem("eg_mm")
        eu_mm = sem("eu_mm")
        silu_done = sem("silu_done")
        ea_ready = sem("ea_ready")
        ea_tr = sem("ea_tr")
        eaT_copied = sem("eaT_copied")
        ed_mm = sem("ed_mm")
        yd_lo = sem("yd_lo")
        yd_hi = sem("yd_hi")
        y_out = [sem(f"y_out{i}") for i in range(2)]
        ygat_in = [sem(f"ygat_in{t}") for t in range(NT)]
        x_moe = sem("x_moe")
        out_store = sem("out_store")
        sp = [{n: sem(f"sp{l}_{n}") for n in (
            "onehot", "idx_mm", "idx", "pad", "rows_in", "w_in", "hg_tr", "hgT", "up_mm", "silu", "a", "a_tr", "aT",
            "down_mm", "y", "stored", "step")} for l in range(L)]

        def releases(key):
            if key[0] == "mod":
                return mod_mm, NMOD * key[1] + key[2] + 1
            if key[0] == "expert":
                _, l, s = key
                done = (eg_mm, eu_mm, ed_mm)[s % 3]
                n = NE * l + NE - 1 + s // 3
                return done, n * (2 if s % 3 == 2 else 1)
            name, l = key
            if name in ("wo0", "wo1"):
                return out_mm, before(out_jobs, l) + len(out_jobs(l))
            if name.startswith("wb"):
                return branch_mm, before(merge_jobs, l) + (int(name[2]) + 1) * 2 * len(queries(l))
            if name.startswith("g"):
                n, half = int(name[1]), int(name[2])
                return gate_mm, before(merge_jobs, l) + (2 * n + half + 1) * len(queries(l))
            n = 0
            for u, tiles in proj_units(l):
                n += tiles
                if u == name:
                    return proj_mm, before(proj_jobs, l) + n

        block = es.enter_context(nc.Block())

        @block.sync
        def _(eng):
            def source(key):
                if key[0] == "mod":
                    return [(slice(0, CW), t_in["w_mod"][key[1], :, CW * key[2]:CW * key[2] + CW])]
                name, l = key
                w = t_in["w_in"][l]
                if name == "kvab":
                    return [(slice(256 * i, 256 * i + 256), w[:, KV_COL[i]:KV_COL[i] + 256]) for i in range(2)]
                col = {"qa": Q_COL[A], "qb": Q_COL[B], "qn": Q_COL[N], "kn": KN_COL, "vn": VN_COL}.get(name)
                if name in ("wo0", "wo1"):
                    w, col = t_in["w_out"][l], CW * int(name[2])
                elif col is None:
                    col = GATE_COL + D * int(name[1]) + CW * int(name[2])
                return [(slice(0, CW), w[:, col:col + CW])]

            def load(key, slot, prev):
                if prev is not None:
                    eng.wait_ge(*releases(prev))
                if key[0].startswith("wb"):
                    src = t_in["w_branch"][key[1], int(key[0][2])].rearrange("(k p) n -> p k n", p=P)
                    eng.dma_start(wdown[slot], src).then_inc(w_in_slot[slot], 16)
                    return
                for cols, src in source(key):
                    eng.dma_start(WR[slot][:, :, cols], src.rearrange("(k p) n -> p k n", p=P))\
                       .then_inc(w_in_slot[slot], 16)

            def expert_source(l, e, j):
                w = t_in[("w_e_gate", "w_e_up", "w_e_down")[j]]
                w = w[l, e] if isinstance(e, int) else w[l, bass.ds(e, 1)].rearrange("o k n -> (o k) n")
                return w.rearrange("(k p) n -> p k n", p=P)

            def load_expert(l, e, parity, j):
                slot = 3 * parity + j
                if isinstance(e, int) and e < 2:
                    eng.wait_ge(*releases(held[l, slot][0]))
                else:
                    n = NE * l + e - 1
                    eng.wait_ge((eg_mm, eu_mm, ed_mm)[j], n * (2 if j == 2 else 1))
                dst = wdown[slot] if j == 2 else WR[slot]
                eng.dma_start(dst, expert_source(l, e, j)).then_inc(w_in_slot[slot], 16)

            for l in range(L):
                for i, (key, slot, prev) in enumerate(sections[l]):
                    if l == 0 and i == 1:
                        eng.wait_ge(c_in, 32)
                        eng.wait_ge(tab_in, 16)
                    if l == 0 and AHEAD <= i < NMOD:
                        eng.wait_ge(mod_mm, i - AHEAD + 1)
                    if key == ("qa", 1):
                        for t in range(NT):
                            eng.wait_ge(ygat_in[t], 32)
                    load(key, slot, prev)
                for e, j in ((0, 0), (0, 1), (1, 0), (1, 1), (0, 2), (2, 0), (2, 1), (1, 2)):
                    load_expert(l, e, e % 2, j)
                with eng.Fori(0, LOOPS) as i:
                    for o in (3, 4):
                        e = 2 * i + o
                        load_expert(l, e, o % 2, 0)
                        load_expert(l, e, o % 2, 1)
                        load_expert(l, e - 1, (o - 1) % 2, 2)
                for e, j in ((NE - 1, 0), (NE - 1, 1), (NE - 2, 2), (NE - 1, 2)):
                    load_expert(l, e, e % 2, j)

                eng.wait_ge(flag_ready, l + 1)
                most = eng.value_load(flag[0:1, 0:1], min_val=0, max_val=NT * P)
                with eng.If(most > CAP):
                    q = sp[l]
                    for i in range(2):
                        eng.wait_ge(y_out[i], 16 * (NE // 2) * (l + 1))
                    with eng.Fori(0, NT - 1) as r:
                        with eng.Fori(0, NE) as e:
                            n = r * NE + e
                            eng.wait_ge(q["onehot"], n + 1)
                            for j in range(3):
                                dst = wdown[2] if j == 2 else WR[j]
                                eng.dma_start(dst, expert_source(l, e, j)).then_inc(q["w_in"], 16)
                    eng.wait_ge(q["w_in"], 48 * NE * (NT - 1))
                    eng.wait_ge(q["stored"], 16 * NE * (NT - 1))

        @block.gpsimd
        def _(eng):
            dma = eng.dma_start
            def load_bmod(l, dst, first):
                n = dst.shape[-1]
                dma(dst, t_in["b_mod"][l, CW * first:CW * first + n].unsqueeze(0).broadcast_to([2, n]))\
                    .then_inc(bmod_in[l], 16)

            def load_norm(l, i):
                dma(nrow[l][i], t_in[("norm1", "norm2")[i]][l].unsqueeze(0).broadcast_to([2, D]))\
                    .then_inc(bmod_in[l], 16)

            def store_mod(l, j):
                i = NMOD * l + j
                eng.wait_ge(mod_row, i + 1)
                dma(mod_d[l, :, CW * j:CW * j + CW], mrow[i % (2 if l else 4)]).then_inc(mod_store[i % 4], 16)

            def mod_stored(count):
                for i in range(4):
                    eng.wait_ge(mod_store[i], 4 * count)

            def load_modb(l, first):
                for s in range(2):
                    for a, part in ((0, first + 1), (1, first)):
                        dma(modb[:, s, a], mod_d[l, s, part * D:(part + 1) * D].unsqueeze(0).broadcast_to([P, D]))\
                            .then_inc(modb_in, 16)

            load_bmod(0, QR[0:2, 0:6 * D], 0)
            load_norm(0, 0)
            load_norm(0, 1)
            for j in range(NMOD):
                store_mod(0, j)
                if j == 3:
                    mod_stored(4)
                    eng.wait_ge(sq_done, NT)
                    load_modb(0, 0)
            dma(masks[:, :], t_in["masks"]).then_inc(const_in, 16)
            dma(tabh[:, :], t_in["tabh"]).then_inc(const_in, 16)
            dma(sink[:, :, :], t_in["sink_b"].unsqueeze(0).broadcast_to([P, L, H])).then_inc(const_in, 16)
            dma(rbias[:, :], t_in["router_bias"].unsqueeze(0).broadcast_to([P, NE])).then_inc(const_in, 16)
            dma(wr[:, :, :], t_in["w_router"].rearrange("(k p) e -> p k e", p=P)).then_inc(const_in, 16)

            def load_gout(l, part):
                for s in range(2):
                    dma(gout[:, s], mod_d[l, s, part * D:(part + 1) * D].unsqueeze(0).broadcast_to([P, D]))\
                        .then_inc(gout_in, 16)

            for l in range(L):
                nq = len(queries(l))
                J0 = before(att_jobs, l)
                for i, name in enumerate(("q_norm_a", "k_norm_a")):
                    dma(gq[:, i], t_in[name][l].unsqueeze(0).broadcast_to([P, DH])).then_inc(gq_in, 16)
                if l == 0:
                    eng.wait_ge(const_in, 80)
                for n in range(NLAT * H):
                    i = n % NBIAS
                    eng.wait_ge(bias_in[i], 32 * ((l * NLAT * H + n) // NBIAS + 1))
                    eng.tensor_tensor(bias[i], bias[i], masks[:, M_COLWIN:M_COLWIN + SEQ],
                                      ALU.add).then_inc(bias_ready, 1)
                eng.wait_ge(pv_mm, J0 + len(att_jobs(l)))
                mod_stored(NMOD * (l + 1))
                load_gout(l, 2)
                load_modb(l, 3)
                if l == 0:
                    eng.wait_ge(y_tr, nq)
                    load_bmod(1, QR[0:2, 4 * D:6 * D], 0)
                    load_bmod(1, KR[0:2, 0:2 * D], 4)
                    load_norm(1, 0)
                for t in range(nq):
                    eng.wait_ge(hn_ready, NT * (2 * l + 1) + t + 1)
                    dma(h2_d[l][P * t:P * t + P], hn[t % 2]).then_inc(h2_store[t % 2], 16)
                eng.wait_ge(x_att, before(out_jobs, l) + 2 * nq)
                load_gout(l, 5)
                if l == 0:
                    for j in range(5):
                        store_mod(1, j)
                    load_norm(1, 1)
                for i in range(2):
                    eng.wait_ge(h2_store[i], 8 * (NT * l + nq))
                eng.wait_ge(idx_ready, l + 1)

                def gather(e):
                    n = NE * l + e
                    if n >= 2:
                        eng.wait_ge(hg_tr, n - 1)
                    eng.indirect_dma_start(hg[e % 2], None, h2_d[l],
                                           bass.IndirectOffsetOnAxis(ap=idx_i[:, e:e + 1], axis=0))\
                        .then_inc(hg_in[e % 2], 16)

                gather(0)
                gather(1)
                if l == 0:
                    for j in range(5, MOD_GAP):
                        store_mod(1, j)
                    eng.wait_ge(flag_ready, 1)
                    load_bmod(1, WK[0:2, 0:2 * D], MOD_GAP)
                    load_modb(1, 0)
                for e in range(NE):
                    if e + 2 < NE:
                        gather(e + 2)
                    eng.wait_ge(yd_lo, NE * l + e + 1)
                    eng.wait_ge(yd_hi, NE * l + e + 1)
                    dma(y_d[l][CAP * e:CAP * e + CAP], yd[e % 2]).then_inc(y_out[e % 2], 16)
                for i in range(2):
                    eng.wait_ge(y_out[i], 16 * (NE // 2) * (l + 1))

                def gather_outputs(table):
                    for t in range(nq):
                        for k in range(2):
                            eng.indirect_dma_start(ygat[t][k], None, table,
                                                   bass.IndirectOffsetOnAxis(ap=slot_i[:, k, t:t + 1], axis=0))\
                                .then_inc(ygat_in[t], 16)

                eng.wait_ge(flag_ready, l + 1)
                most = eng.value_load(flag[0:1, 0:1], min_val=0, max_val=NT * P)
                with eng.If(most > CAP):
                    q = sp[l]
                    with eng.Fori(0, NT - 1) as r:
                        with eng.Fori(0, NE) as e:
                            n = r * NE + e
                            eng.wait_ge(q["idx"], n + 1)
                            eng.tensor_tensor(sp_pad[:, :], rbias[:, 0:1], rbias[:, 0:1], ALU.add).then_inc(q["pad"], 1)
                            eng.indirect_dma_start(hg[0], None, h2_d[l],
                                                   bass.IndirectOffsetOnAxis(ap=sp_idx[:, 0:1], axis=0))\
                                .then_inc(q["rows_in"], 16)
                            eng.wait_ge(q["pad"], n + 1)
                            eng.wait_ge(q["y"], n + 1)
                            row = r * PASS + e * CAP + PASS
                            dma(y_d[l][bass.ds(row, CAP)], yd[0]).then_inc(q["stored"], 16)
                            eng.wait_ge(q["stored"], 16 * (n + 1))

                    gather_outputs(y_d[l])
                with eng.If(most <= CAP):
                    gather_outputs(y_d[l][0:PASS])
                if l == 0:
                    for j in range(MOD_GAP, NMOD):
                        store_mod(1, j)

            dma(modb[:, 0, 0], t_in["final_norm"].unsqueeze(0).broadcast_to([P, D])).then_inc(const_in, 16)
            for t in range(NLAT):
                eng.wait_ge(hn_ready, NT * 3 + NLAT + t + 1)
                dma(out[0, P * t:P * t + P], hn[t % 2]).then_inc(out_store, 16)
            eng.wait_ge(out_store, 16 * NLAT)

        @block.scalar
        def _(eng):
            act = eng.activation
            eng.dma_start(crow[0:1], c).then_inc(c_in, 16)
            eng.dma_start(crow[1:2], c_ctx.unsqueeze(0)).then_inc(c_in, 16)
            eng.dma_start(tab[:, :], t_in["tab"]).then_inc(tab_in, 16)
            eng.wait_ge(cT_mm, 1)
            act(cT[:, :, :].rearrange("p k s -> p (k s)"), bank[7][:, 0:2 * KD], ACT.Silu).then_inc(cT_ready, 1)
            for t in range(NLAT):
                eng.dma_start(X[:, t], x[0, P * t:P * t + P]).then_inc(x_in, 16)
            for t in range(NLAT):
                eng.dma_start(X[:, NLAT + t], ctx_in[0, P * t:P * t + P]).then_inc(x_in, 16)

            n_norm = 0

            def norm_root(t, squares):
                nonlocal n_norm
                act(squares[t], X[:, t], ACT.Square, accum_out=ssq[:, t:t + 1]).then_inc(sq_done, 1)
                n_norm += 1
                eng.wait_ge(sq_done, n_norm)
                act(rms[:, t:t + 1], ssq[:, t:t + 1], ACT.Sqrt, bias=tab[:, T_EPS:T_EPS + 1], scale=1.0 / D)\
                    .then_inc(rms_done, 1)

            def copy_h(n, t):
                eng.wait_ge(h_tr, n + 1)
                for g in range(2):
                    src = bank[4 + 2 * (t % 2) + g][:, :].rearrange("p (k q) -> p k q", k=4)
                    act(HT[:, 4 * g:4 * g + 4, P * t:P * t + P], src, ACT.Copy).then_inc(h_copied, 1)

            n_sq = 0
            n_nat = 0
            n_v = 0
            for l in range(L):
                nq = len(queries(l))
                if l == 0:
                    eng.wait_ge(tab_in, 16)
                    eng.wait_ge(x_in, 16 * NT)
                for t in range(NT):
                    if l:
                        eng.wait_ge(x_moe, t + 1)
                    norm_root(t, junk[2 * l])
                    if l and t:
                        copy_h(NT * 2 * l + t - 1, t - 1)
                for t in range(NT - 1 if l else 0, NT):
                    copy_h(NT * 2 * l + t, t)
                for i in range(4):
                    eng.wait_ge(mod_store[i], 4 * NMOD * (l + 1))

                jobs = proj_jobs(l)
                late = []

                def copy_nat(u, t):
                    nonlocal n_nat
                    eng.wait_ge(nat_tr, n_nat + 1)
                    src = bank[4 + n_nat % 2][:, :].rearrange("p (j q) -> p j q", j=4)
                    cols = slice(P * t, P * t + P)
                    if u == "kvab":
                        dst = KR[:, 0:1024].rearrange("p (j n) -> p j n", j=2)[:, :, cols]
                        act(dst, src[:, 0:2], ACT.Copy).then_inc(nat_copied, 1)
                    else:
                        dst = kT[N] if u == "kn" else qT["abn".index(u[1])]
                        act(dst[:, :, cols], src, ACT.Copy).then_inc(nat_copied, 1)
                    n_nat += 1

                for j, (u, t) in enumerate(jobs):
                    n = before(proj_jobs, l) + j
                    pb = bank[j % 4]
                    if u in ("kvab", "qa"):
                        eng.wait_ge(proj_mm, n + 1)
                        if n_sq:
                            eng.wait_ge(hms_done, n_sq)
                        w = P if u == "kvab" else BW
                        act(hsq[:, 0:w], pb[:, 0:w], ACT.Square).then_inc(hsq_done, 1)
                        n_sq += 1
                    if u == "kvab":
                        v = pb[:, :].rearrange("p (b c n) -> p b c n", b=2, c=2)[:, :, 1]
                        act(vAB[:, t], v, ACT.Copy).then_inc(v_used, 1)
                        n_v += 1
                    if u == "vn":
                        eng.wait_ge(proj_mm, n + 1)
                        act(vN[:, t], pb[:, :], ACT.Copy).then_inc(v_used, 1)
                        n_v += 1
                    if u in ("kvab", "qa"):
                        eng.wait_ge(hms_done, n_sq)
                        k = 2 if u == "kvab" else H
                        act(hrt[:, 0:k], hss[:, 0:k], ACT.Sqrt).then_inc(hrt_done, 1)
                    late.append((u, t))
                    if len(late) > 2:
                        job = late.pop(0)
                        if job[0] != "vn":
                            copy_nat(*job)
                for job in late:
                    if job[0] != "vn":
                        copy_nat(*job)

                jobs = att_jobs(l)
                J0 = before(att_jobs, l)
                M = len(jobs)
                at_n = jobs.index((N, 0, 0))

                def load_bias(n):
                    t, h = divmod(n, H)
                    for half in range(2):
                        r = 2 * t + half
                        dst = bias[n % NBIAS][GRID_W * half:GRID_W * half + GRID_W].rearrange("c (i k) -> c i k", i=4)
                        eng.dma_start(dst, t_in["rpb"][l, h, 7 - r:11 - r].rearrange("i c k -> c i k"))\
                            .then_inc(bias_in[n % NBIAS], 16)

                for n in range(NBIAS):
                    load_bias(n)
                for s in range(M + 5):
                    n = s - at_n + NBIAS - 1
                    if NBIAS <= n < NLAT * H:
                        eng.wait_ge(nm_ready, J0 + s)
                        load_bias(n)
                    d = s - 3
                    if 0 <= d < M:
                        b, t, h = jobs[d]
                        ks = slice(0, NT) if t < NLAT else slice(NLAT, NT)
                        eng.wait_ge(pt_tr, J0 + d + 1)
                        if J0 + d >= 2:
                            eng.wait_ge(pv_mm, J0 + d - 1)
                        i = (J0 + d) % 2
                        act(PT[i][:, ks], bank[3 + i][:, :].rearrange("p (k q) -> p k q", k=4)[:, ks], ACT.Copy)\
                            .then_inc(pt_copied[i], 1)
                    if s < M:
                        a = J0 + s
                        b, t, h = jobs[s]
                        g = (J0 + s) // H
                        w = slice(0 if t < NLAT else SEQ, CW + 1 if b == B else CW)
                        eng.wait_ge(nm_ready, a + 1)
                        if s >= 4:
                            eng.wait_ge(pt_tr, a - 3)
                        src = S[a % 2] if biased(b, t) else sbank[a % 4]
                        act(probs[a % 4][:, w], src[:, w], ACT.Exp, bias=nmx[:, a % 4:a % 4 + 1],
                            accum_out=psm[:, a % 4:a % 4 + 1]).then_inc(exp_done, 1)
                    d = s - 5
                    if 0 <= d < M and jobs[d][2] == H - 1:
                        b, t, _ = jobs[d]
                        g = (J0 + d) // H
                        eng.wait_ge(pv_mm, J0 + d + 1)
                        act(qT[b][:, :, P * t:P * t + P], bank[5 + g % 2][:, :].rearrange("p (j q) -> p j q", j=4),
                            ACT.Copy).then_inc(o_copied, 1)

                for i, (n, half, t) in enumerate(merge_jobs(l)):
                    i += before(merge_jobs, l)
                    eng.wait_ge(gate_mm, i + 1)
                    if i >= 2:
                        eng.wait_ge(merged, i - 1)
                    act(sg[i % 2], bank[i % 2][:, :], ACT.Sigmoid).then_inc(sig_ready, 1)
                for t in range(nq):
                    eng.wait_ge(y_tr, (NT * l) + t + 1)
                    for g in range(2):
                        src = bank[4 + 2 * (t % 2) + g][:, :].rearrange("p (k q) -> p k q", k=4)
                        act(HT[:, 4 * g:4 * g + 4, P * t:P * t + P], src, ACT.Copy).then_inc(y_copied, 1)

                for t in range(nq):
                    eng.wait_ge(x_att, before(out_jobs, l) + 2 * (t + 1))
                    norm_root(t, junk[1])
                    if t:
                        copy_h(NT * (2 * l + 1) + t - 1, t - 1)
                copy_h(NT * (2 * l + 1) + nq - 1, nq - 1)
                eng.wait_ge(router_mm, l + 1)
                act(r_sc[:, 0:nq].rearrange("p t e -> p (t e)"), bank[3][:, 0:nq * NE], ACT.Sigmoid)\
                    .then_inc(score_ready, 1)

                def copy_hgT(n, parity):
                    eng.wait_ge(hg_tr, n + 1)
                    if not isinstance(n, int) or n >= 2:
                        eng.wait_ge(eu_mm, n - 1)
                    for g in range(2):
                        src = bank[6 + g][:, :].rearrange("p (k q) -> p k q", k=4)
                        act(hgT[parity][:, 4 * g:4 * g + 4], src, ACT.Copy).then_inc(hgT_copied, 1)

                def silu(n):
                    eng.wait_ge(eg_mm, n + 1)
                    eng.wait_ge(ea_ready, n)
                    act(esg, bank[0][:, :], ACT.Silu).then_inc(silu_done, 1)

                def store_hi(n, parity):
                    eng.wait_ge(ed_mm, 2 * n + 2)
                    if not isinstance(n, int) or n >= 2:
                        eng.wait_ge(y_out[parity], (n - parity) * 8)
                    act(yd[parity][:, CW:D], bank[5][:, :], ACT.Copy).then_inc(yd_hi, 1)

                E0 = NE * l
                def step(n, o):
                    silu(n)
                    copy_hgT(n + 1, (o + 1) % 2)
                    store_hi(n - 1, (o - 1) % 2)

                copy_hgT(E0, 0)
                silu(E0)
                copy_hgT(E0 + 1, 1)
                step(E0 + 1, 1)
                step(E0 + 2, 2)
                with eng.Fori(0, LOOPS) as i:
                    for o in (3, 4):
                        step(E0 + 2 * i + o, o)
                silu(E0 + NE - 1)
                store_hi(E0 + NE - 2, 0)
                store_hi(E0 + NE - 1, 1)

                eng.wait_ge(flag_ready, l + 1)
                most = eng.value_load(flag[0:1, 0:1], min_val=0, max_val=NT * P)
                with eng.If(most > CAP):
                    q = sp[l]
                    for i in range(2):
                        eng.wait_ge(y_out[i], 16 * (NE // 2) * (l + 1))
                    with eng.Fori(0, (NT - 1) * NE) as n:
                        eng.wait_ge(q["hg_tr"], n + 1)
                        for g in range(2):
                            src = bank[6 + g][:, :].rearrange("p (k q) -> p k q", k=4)
                            act(hgT[0][:, 4 * g:4 * g + 4], src, ACT.Copy).then_inc(q["hgT"], 1)
                        eng.wait_ge(q["up_mm"], n + 1)
                        act(esg, bank[0][:, :], ACT.Silu).then_inc(q["silu"], 1)

            for t in range(NLAT):
                eng.wait_ge(x_moe, NT + t + 1)
                norm_root(t, junk[2])

        @block.vector
        def _(eng):
            tt, ts, stt = eng.tensor_tensor, eng.tensor_scalar, eng.scalar_tensor_tensor
            steps = [0]

            def link(ins):
                ins.then_inc(dve_step, 1)
                steps[0] += 1
                eng.wait_ge(dve_step, steps[0])


            def mod_rows(i):
                l, j = divmod(i, NMOD)
                if j == 0:
                    eng.wait_ge(bmod_in[l], 16 * 3)
                if i == NMOD + MOD_GAP:
                    eng.wait_ge(bmod_in[l], 16 * 5)
                eng.wait_ge(mod_mm, i + 1)
                n = 2 if l else 4
                if i >= n:
                    eng.wait_ge(mod_store[(i - n) % 4], 16 * ((i - n) // 4 + 1))
                row, b, made = mrow[i % n], bmod[i], bank[MOD_BANK[i]][0:2, :]
                part, half = divmod(j, 2)
                if part in (1, 4):
                    link(tt(row, made, b, ALU.add))
                    stt(row, row, 1.0, nrow[l][part // 4][:, CW * half:CW * half + CW], ALU.add, ALU.mult)\
                        .then_inc(mod_row, 1)
                else:
                    tt(row, made, b, ALU.add).then_inc(mod_row, 1)

            n_hn = 0

            n_norm = 0

            def inverse_root(t):
                nonlocal n_norm
                n_norm += 1
                eng.wait_ge(rms_done, n_norm)
                link(eng.reciprocal(rstd[:, t:t + 1], rms[:, t:t + 1]))

            def modulated(t):
                nonlocal n_hn
                s = 0 if t < NLAT else 1
                inverse_root(t)
                if n_hn >= 2:
                    eng.wait_ge(h_tr, n_hn - 1)
                link(stt(hn[t % 2], X[:, t], rstd[:, t:t + 1], modb[:, s, 0], ALU.mult, ALU.mult))
                tt(hn[t % 2], hn[t % 2], modb[:, s, 1], ALU.add).then_inc(hn_ready, 1)
                n_hn += 1

            n_hsq, n_nat = 0, 0
            for i in range(NMOD):
                mod_rows(i)
                if i in H1_ROWS:
                    t = H1_ROWS.index(i)
                    if t == 0:
                        eng.wait_ge(modb_in, 64)
                    modulated(t)
            eng.wait_ge(tab_in, 16)
            for l in range(L):
                nq = len(queries(l))

                eng.wait_ge(gq_in, 32 * (l + 1))

                def heads(v, k):
                    return v.rearrange("p (h d) -> p h d", h=k)

                def normed(pb, k, gain, scale_in_root):
                    nonlocal n_hsq
                    eng.wait_ge(hsq_done, n_hsq + 1)
                    link(eng.tensor_reduce(hss[:, 0:k], heads(hsq[:, 0:k * DH], k), AX, ALU.add))
                    if scale_in_root:
                        ts(hss[:, 0:k], hss[:, 0:k], DH * EPS, None, ALU.add).then_inc(hms_done, 1)
                    else:
                        ts(hss[:, 0:k], hss[:, 0:k], 1.0 / DH, EPS, ALU.mult, ALU.add).then_inc(hms_done, 1)
                    n_hsq += 1
                    eng.wait_ge(hrt_done, n_hsq)
                    link(eng.reciprocal(hrs[:, 0:k], hrt[:, 0:k]))
                    o = heads(hn_a[:, 0:k * DH], k)
                    link(tt(o, heads(pb, k), hrs[:, 0:k].unsqueeze(2).broadcast_to([P, k, DH]), ALU.mult))
                    return o, gq[:, gain].unsqueeze(1).broadcast_to([P, k, DH])

                def rotate(v, k, t, dst, view):
                    r1, r2 = rope1[:, 0:k * DH], rope2[:, 0:k * DH]
                    cos = tab[:, T_ROPEC + DH * t:T_ROPEC + DH * t + DH].unsqueeze(1).broadcast_to([P, k, DH])
                    tt(heads(r1, k), heads(v, k), cos, ALU.mult)
                    v5 = v.rearrange("p (h a x i) -> p h a x i", a=2, x=2, i=16)
                    o5 = r2.rearrange("p (h a x i) -> p h a x i", a=2, x=2, i=16)
                    for xx in range(2):
                        c0 = T_ROPES + DH * t + 32 * xx
                        sin = tab[:, c0:c0 + 32].rearrange("p (a i) -> p a i", a=2).unsqueeze(1)\
                            .broadcast_to([P, k, 2, 16])
                        ins = tt(o5[:, :, :, xx], v5[:, :, :, 1 - xx], sin, ALU.mult)
                    link(ins)
                    return tt(view(dst, False), view(r1, True), view(r2, True), ALU.add)

                def pair_view(v, source):
                    if source:
                        return v.rearrange("p (g j d) -> p g j d", g=2, j=4)
                    return v.rearrange("p (j g d) -> p g j d", g=2, j=4)

                def same_view(v, source):
                    return v

                for j, (u, t) in enumerate(proj_jobs(l)):
                    n = before(proj_jobs, l) + j
                    pb = bank[j % 4]
                    if u == "vn":
                        continue
                    eng.wait_ge(proj_mm, n + 1)
                    if n_nat >= 2:
                        eng.wait_ge(nat_tr, n_nat - 1)
                    dst = nat[n_nat % 2]
                    if u == "kvab":
                        o, gain = normed(pb[:, 0:P], 2, 1, False)
                        if t < NLAT:
                            link(tt(o, o, gain, ALU.mult))
                            link(rotate(hn_a[:, 0:P], 2, t, dst[:, 0:P], same_view))
                            link(eng.tensor_copy(hn_a[:, P:2 * P], pb[:, 2 * P:3 * P]))
                            last = rotate(hn_a[:, P:2 * P], 2, t, dst[:, P:2 * P], same_view)
                        else:
                            tt(heads(dst[:, 0:P], 2), o, gain, ALU.mult)
                            last = eng.tensor_copy(dst[:, P:2 * P], pb[:, 2 * P:3 * P])
                    elif u == "qa":
                        o, gain = normed(pb[:, :], H, 0, True)
                        if t < NLAT:
                            link(tt(o, o, gain, ALU.mult))
                            last = rotate(hn_a, H, t, dst, pair_view)
                        else:
                            link(tt(o, o, gain, ALU.mult))
                            last = eng.tensor_copy(pair_view(dst, False), pair_view(hn_a, True))
                    elif u == "qb":
                        if t < NLAT:
                            link(ts(hn_a, pb[:, :], DH ** -0.5, None, ALU.mult))
                            last = rotate(hn_a, H, t, dst, pair_view)
                        else:
                            last = ts(pair_view(dst, False), pair_view(pb[:, :], True), DH ** -0.5, None, ALU.mult)
                    elif u == "qn":
                        last = ts(dst, pb[:, :], DH ** -0.5, None, ALU.mult)
                    else:
                        last = eng.tensor_copy(dst, pb[:, :])
                    last.then_inc(nat_ready, 1)
                    n_nat += 1
                    eng.wait_ge(nat_ready, n_nat)

                if l == 0:
                    eng.wait_ge(const_in, 80)
                jobs = att_jobs(l)
                J0 = before(att_jobs, l)
                M = len(jobs)
                n_bias = l * NLAT * H
                for s in range(M + 3):
                    if s < M:
                        a = J0 + s
                        b, t, h = jobs[s]
                        nm, bk = nmx[:, a % 4:a % 4 + 1], sbank[a % 4]
                        first = 0 if t < NLAT else SEQ
                        eng.wait_ge(qk_mm, a + 1)
                        if not biased(b, t):
                            eng.tensor_reduce(nm, bk[:, first:CW], AX, ALU.max, negate=True).then_inc(nm_ready, 1)
                        else:
                            if s >= 2:
                                eng.wait_ge(exp_done, a - 1)
                            dst, m1, m2 = S[a % 2], mx[:, a % 4:a % 4 + 1], mx2[:, a % 4:a % 4 + 1]
                            if b == B:
                                eng.tensor_copy(dst[:, CW:CW + 1], sink[:, l, h:h + 1])
                                k, add, start = slice(first, CW), M_BAND + CW * (t % NLAT), sink[:, l, h:h + 1]
                                add = masks[:, add + first:add + CW]
                            else:
                                n_bias += 1
                                link(eng.tensor_tensor_reduce(out=dst[:, SEQ:CW], in0=bk[:, SEQ:CW],
                                                              in1=masks[:, M_BAND + SEQ:M_BAND + CW], scale=1.0,
                                                              scalar=-3e38, op0=ALU.add, op1=ALU.max, accum_out=m2))
                                eng.wait_ge(bias_ready, n_bias)
                                k, add, start = slice(0, SEQ), bias[(n_bias - 1) % NBIAS], m2
                            link(eng.tensor_tensor_reduce(out=dst[:, k], in0=bk[:, k], in1=add, scale=1.0,
                                                          scalar=start, op0=ALU.add, op1=ALU.max, accum_out=m1))
                            ts(nm, m1, -1.0, None, ALU.mult).then_inc(nm_ready, 1)
                    d = s - 1
                    if 0 <= d < M:
                        a = J0 + d
                        b, t, h = jobs[d]
                        eng.wait_ge(exp_done, a + 1)
                        link(eng.reciprocal(rcp[:, a % 4:a % 4 + 1], psm[:, a % 4:a % 4 + 1]))
                        w = slice(0 if t < NLAT else SEQ, CW)
                        ts(probs[a % 4][:, w], probs[a % 4][:, w], rcp[:, a % 4:a % 4 + 1], None, ALU.mult)\
                            .then_inc(p_norm, 1)
                eng.wait_ge(pv_mm, J0 + M)

                for i, (n, half, t) in enumerate(merge_jobs(l)):
                    i += before(merge_jobs, l)
                    eng.wait_ge(sig_ready, i + 1)
                    eng.wait_ge(branch_mm, i + 1)
                    y = Y[:, t, CW * half:CW * half + CW]
                    if n == 0:
                        tt(y, sg[i % 2], bank[2 + i % 2][:, :], ALU.mult).then_inc(merged, 1)
                    else:
                        link(tt(wtmp[i % 2], sg[i % 2], bank[2 + i % 2][:, :], ALU.mult))
                        tt(y, y, wtmp[i % 2], ALU.add).then_inc(merged, 1)
                eng.wait_ge(merged, before(merge_jobs, l) + len(merge_jobs(l)))

                eng.wait_ge(gout_in, 32 * (2 * l + 1))
                for i, (t, half) in enumerate(out_jobs(l)):
                    n = before(out_jobs, l) + i
                    s = 0 if t < NLAT else 1
                    cols = slice(CW * half, CW * half + CW)
                    eng.wait_ge(out_mm, n + 1)
                    made = bank[i % 3][:, :]
                    link(tt(made, made, gout[:, s, cols], ALU.mult))
                    tt(X[:, t, cols], X[:, t, cols], made, ALU.add).then_inc(x_att, 1)
                    if half == 1:
                        if t == 0:
                            eng.wait_ge(modb_in, 64 * (2 * l + 2))
                        if t >= 2:
                            eng.wait_ge(h2_store[t % 2], 8 * NT * l + 16)
                        modulated(t)
                eng.wait_ge(x_att, before(out_jobs, l) + 2 * nq)

                def bc(v, k):
                    return v.unsqueeze(2).broadcast_to([P, nq, k])

                R = [P, nq, NE]
                sc, sel, key, o1, o2, pos = (v[:, 0:nq] for v in (r_sc, r_sel, r_key, r_o1, r_o2, r_pos))
                rank = tab[:, T_RANK:T_RANK + NE].unsqueeze(1).broadcast_to(R)
                rank4 = tab[:, T_RANK:T_RANK + NG].unsqueeze(1).broadcast_to([P, nq, NG])
                eng.wait_ge(score_ready, l + 1)
                link(tt(sel, sc, rbias[:, :].unsqueeze(1).broadcast_to(R), ALU.add))
                g4 = sel.rearrange("p t (g e) -> p (t g) e", g=NG)
                pr = r_pair[:, 0:nq * NG]
                tt(pr[:, :, 0:3], g4[:, :, 0:3], g4[:, :, 1:4], ALU.add)
                tt(pr[:, :, 3:5], g4[:, :, 0:2], g4[:, :, 2:4], ALU.add)
                link(tt(pr[:, :, 5:6], g4[:, :, 0:1], g4[:, :, 3:4], ALU.add))
                gs, gk, m, m2 = r_g[:, 0:nq], r_gk[:, 0:nq], r_m[:, 0:nq], r_n[:, 0:nq]
                link(eng.tensor_reduce(gs.rearrange("p t g -> p (t g)"), pr, AX, ALU.max))
                link(eng.tensor_reduce(m, gs, AX, ALU.max))
                link(tt(gs, gs, bc(m, NG), ALU.is_equal))
                link(tt(gk, gs, rank4, ALU.mult))
                link(eng.tensor_reduce(m, gk, AX, ALU.max))
                link(tt(gs, gk, bc(m, NG), ALU.is_equal))
                link(ts(gk, gs, -1.0, -NEG, ALU.add, ALU.mult))

                def per_group(v):
                    return v.rearrange("p t g -> p (t g)").unsqueeze(2).broadcast_to([P, nq * NG, NG])

                link(tt(g4, g4, per_group(gs), ALU.mult))
                link(tt(g4, g4, per_group(gk), ALU.add))
                for k, o in enumerate((o1, o2)):
                    link(eng.tensor_reduce(m, sel, AX, ALU.max))
                    link(tt(o, sel, bc(m, NE), ALU.is_equal))
                    link(tt(key, o, rank, ALU.mult))
                    link(eng.tensor_reduce(m, key, AX, ALU.max))
                    link(tt(o, key, bc(m, NE), ALU.is_equal))
                    if k == 0:
                        link(stt(sel, o, 2 * NEG, sel, ALU.mult, ALU.add))
                link(tt(key, o1, o2, ALU.add))
                eng.tensor_copy(selh[:, 0:nq], key).then_inc(sel_ready, 1)
                if l == 0:
                    for i in range(3):
                        mod_rows(NMOD + i)
                eng.wait_ge(pos_mm, l + 1)
                link(eng.tensor_reduce(cnt[:, :], bank[1][:, nq * NE:nq * NE + NE], AX, ALU.max))
                link(eng.tensor_copy(pos.rearrange("p t e -> p (t e)"), bank[1][:, 0:nq * NE]))
                link(stt(posm[:, 0:nq], pos, 1.0, key, ALU.add, ALU.mult))
                link(ts(posm[:, 0:nq], posm[:, 0:nq], -1.0, None, ALU.add))
                iota = tab[:, T_IOTA:T_IOTA + P]
                for t in range(nq):
                    tt(oneh[t].rearrange("p (e j) -> p e j", e=NE), iota.unsqueeze(1).broadcast_to([P, NE, P]),
                       posm[:, t].unsqueeze(2).broadcast_to([P, NE, P]), ALU.is_equal).then_inc(oneh_ready, 1)
                if l == 0:
                    mod_rows(NMOD + 3)
                    mod_rows(NMOD + 4)
                eng.wait_ge(idx_mm, l + 1)
                eng.tensor_copy(idx_i[:, :], bank[2][:, 0:NE]).then_inc(idx_ready, 1)
                for k, o in enumerate((o1, o2)):
                    link(tt(sel, sc, o, ALU.mult))
                    link(eng.tensor_reduce(r_w[:, 0:nq, k], sel, AX, ALU.add))
                link(tt(m, r_w[:, 0:nq, 0], r_w[:, 0:nq, 1], ALU.add))
                link(eng.reciprocal(m2, m))
                link(tt(r_w[:, 0:nq], r_w[:, 0:nq], bc(m2, 2), ALU.mult))
                ebase = tab[:, T_EBASE:T_EBASE + NE].unsqueeze(1).broadcast_to(R)
                link(ts(key, pos, float(CAP), None, ALU.is_ge))
                for r in range(2, NT):
                    link(stt(key, pos, float(CAP * r), key, ALU.is_ge, ALU.add))
                link(stt(pos, key, float(PASS - CAP), pos, ALU.mult, ALU.add))
                link(tt(pos, pos, ebase, ALU.add))
                for k, o in enumerate((o1, o2)):
                    link(tt(key, pos, o, ALU.mult))
                    link(eng.tensor_reduce(slotf[:, 0:nq, k], key, AX, ALU.add))
                    link(eng.tensor_copy(slot_i[:, k, 0:nq], slotf[:, 0:nq, k]))
                eng.tensor_copy(flag[:, :], cnt[:, :]).then_inc(flag_ready, 1)
                if l == 0:
                    for i in range(5, MOD_GAP):
                        mod_rows(NMOD + i)

                def gated(n):
                    eng.wait_ge(silu_done, n + 1)
                    eng.wait_ge(eu_mm, n + 1)
                    eng.wait_ge(ea_tr, n)
                    tt(ea, esg, bank[1][:, :], ALU.mult).then_inc(ea_ready, 1)

                def store_lo(n, parity):
                    eng.wait_ge(ed_mm, 2 * n + 1)
                    if not isinstance(n, int) or n >= 2:
                        eng.wait_ge(y_out[parity], (n - parity) * 8)
                    eng.tensor_copy(yd[parity][:, 0:CW], bank[4][:, :]).then_inc(yd_lo, 1)

                def copy_eaT(n):
                    eng.wait_ge(ea_tr, n + 1)
                    eng.tensor_copy(eaT, bank[2][:, :].rearrange("p (k q) -> p k q", k=4)).then_inc(eaT_copied, 1)

                E0 = NE * l
                def step(n, o):
                    gated(n)
                    store_lo(n - 1, (o - 1) % 2)
                    copy_eaT(n)

                gated(E0)
                copy_eaT(E0)
                step(E0 + 1, 1)
                step(E0 + 2, 2)
                with eng.Fori(0, LOOPS) as i:
                    for o in (3, 4):
                        step(E0 + 2 * i + o, o)
                gated(E0 + NE - 1)
                store_lo(E0 + NE - 2, 0)
                copy_eaT(E0 + NE - 1)
                store_lo(E0 + NE - 1, 1)

                eng.wait_ge(flag_ready, l + 1)
                most = eng.value_load(flag[0:1, 0:1], min_val=0, max_val=NT * P)
                with eng.If(most > CAP):
                    q = sp[l]
                    for i in range(2):
                        eng.wait_ge(y_out[i], 16 * (NE // 2) * (l + 1))
                    with eng.Fori(0, NT - 1) as r:
                        ts(posm[:, 0:nq], posm[:, 0:nq], -float(CAP), None, ALU.add).then_inc(q["step"], 1)
                        with eng.Fori(0, NE) as e:
                            n = r * NE + e
                            eng.wait_ge(q["step"], r + 1)
                            for t in range(nq):
                                ins = ts(sp_oh[:, t], iota, posm[:, t, bass.ds(e, 1)], None, ALU.is_equal)
                            ins.then_inc(q["onehot"], 1)
                            eng.wait_ge(q["idx_mm"], n + 1)
                            eng.tensor_copy(sp_idx[:, :], bank[2][:, 0:1]).then_inc(q["idx"], 1)
                            eng.wait_ge(q["silu"], n + 1)
                            tt(ea, esg, bank[1][:, :], ALU.mult).then_inc(q["a"], 1)
                            eng.wait_ge(q["a_tr"], n + 1)
                            eng.tensor_copy(eaT, bank[3][:, :].rearrange("p (k q) -> p k q", k=4))\
                                .then_inc(q["aT"], 1)
                            eng.wait_ge(q["down_mm"], n + 1)
                            eng.tensor_copy(yd[0][:, 0:CW], bank[4][:, :])
                            eng.tensor_copy(yd[0][:, CW:D], bank[5][:, :]).then_inc(q["y"], 1)
                            eng.wait_ge(q["stored"], 16 * n + 16)

                eng.wait_ge(gout_in, 32 * (2 * l + 2))
                def add_experts(t):
                    eng.wait_ge(ygat_in[t], 32 * (l + 1))
                    y0, y1 = ygat[t]
                    link(ts(y0, y0, r_w[:, t, 0:1], None, ALU.mult))
                    link(stt(y0, y1, r_w[:, t, 1:2], y0, ALU.mult, ALU.add))
                    link(tt(y0, y0, gout[:, 0 if t < NLAT else 1], ALU.mult))
                    tt(X[:, t], X[:, t], y0, ALU.add).then_inc(x_moe, 1)
                    eng.wait_ge(x_moe, NT * l + t + 1)

                if l == 0:
                    for t in range(NT):
                        if t < 2:
                            mod_rows(NMOD + MOD_GAP + t)
                        add_experts(t)
                        if t == 1:
                            eng.wait_ge(modb_in, 64 * 3)
                        if t:
                            modulated(t - 1)
                        if t == 1:
                            mod_rows(2 * NMOD - 2)
                            mod_rows(2 * NMOD - 1)
                    modulated(NT - 1)
                else:
                    for t in range(NLAT):
                        add_experts(t)

            eng.wait_ge(const_in, 96)
            for t in range(NLAT):
                inverse_root(t)
                stt(hn[t], X[:, t], rstd[:, t:t + 1], modb[:, 0, 0], ALU.mult, ALU.mult).then_inc(hn_ready, 1)

        @block.tensor
        def _(eng):
            mm = eng.matmul

            def arrived(key):
                slot, n = landed[key]
                eng.wait_ge(w_in_slot[slot], n)
                return slot

            eng.wait_ge(c_in, 32)
            eng.wait_ge(tab_in, 16)
            for k in range(KD):
                ins = mm(bank[7][:, 2 * k:2 * k + 2], crow[:, P * k:P * k + P], tab[0:2, T_IDENT:T_IDENT + 2],
                         start=True, stop=True, is_transpose=True)
            ins.then_inc(cT_mm, 1)
            eng.wait_ge(cT_ready, 1)
            n_h = 0

            def transposes(src, dst, count):
                for k in range(count):
                    ins = mm(dst[:, P * k:P * k + P], src[:, P * k:P * k + P], ident,
                             start=True, stop=True, is_transpose=True)
                return ins

            def transpose_h(t):
                nonlocal n_h
                eng.wait_ge(hn_ready, n_h + 1)
                if n_h >= 2 and t >= 2:
                    eng.wait_ge(h_copied, 2 * (n_h - 1))
                for g in range(2):
                    ins = transposes(hn[t % 2][:, CW * g:CW * g + CW], bank[4 + 2 * (t % 2) + g], 4)
                ins.then_inc(h_tr, 1)
                n_h += 1

            def modulation(i):
                slot, use = arrived(("mod", *divmod(i, NMOD))), MOD_BANK[i]
                before_it = [k for k in range(i) if MOD_BANK[k] == use]
                if before_it:
                    eng.wait_ge(mod_row, before_it[-1] + 1)
                for k in range(KD):
                    ins = mm(bank[use][0:2, :], cT[:, k, :], WR[slot][:, k], start=(k == 0), stop=(k == KD - 1))
                ins.then_inc(mod_mm, 1)

            for i in range(NMOD):
                modulation(i)
                if i - 2 in H1_ROWS:
                    transpose_h(H1_ROWS.index(i - 2))
            for t in range(NT):
                if H1_ROWS[t] + 2 >= NMOD:
                    transpose_h(t)

            n_nat, n_v, n_all_att = 0, 0, 0
            for l in range(L):
                nq = len(queries(l))
                if l:
                    eng.wait_ge(yd_lo, NE * l)
                    eng.wait_ge(yd_hi, NE * l)
                    transpose_h(0)

                jobs = proj_jobs(l)
                n_nat0, n_v0 = n_nat, n_v

                def transpose_nat(u):
                    nonlocal n_nat
                    eng.wait_ge(nat_ready, n_nat + 1)
                    if n_nat - n_nat0 >= 2:
                        eng.wait_ge(nat_copied, n_nat - 1)
                    transposes(nat[n_nat % 2], bank[4 + n_nat % 2], 2 if u == "kvab" else 4).then_inc(nat_tr, 1)
                    n_nat += 1

                for j, (u, t) in enumerate(jobs):
                    slot = arrived((u, l))
                    if j < NT:
                        if l and j == 1:
                            transpose_h(1)
                        if l and j == 2:
                            transpose_h(2)
                            transpose_h(3)
                        eng.wait_ge(h_copied, 2 * (NT * 2 * l + t + 1))
                        eng.wait_ge(mod_row, NMOD * (l + 1) - 3 + j)
                    if j >= 4:
                        past = jobs[:j - 3]
                        nats = sum(x[0] != "vn" for x in past)
                        vs = sum(x[0] in ("vn", "kvab") for x in past)
                        eng.wait_ge(nat_ready, n_nat0 + nats)
                        eng.wait_ge(v_used, n_v0 + vs)
                    for k in range(KD):
                        ins = mm(bank[j % 4][:, :], HT[:, k, P * t:P * t + P], WR[slot][:, k],
                                 start=(k == 0), stop=(k == KD - 1))
                    ins.then_inc(proj_mm, 1)
                    if j >= 2 and jobs[j - 2][0] != "vn":
                        transpose_nat(jobs[j - 2][0])
                for u, _ in jobs[-2:]:
                    if u != "vn":
                        transpose_nat(u)
                n_v = n_v0 + 2 * NT
                eng.wait_ge(v_used, n_v)
                eng.wait_ge(nat_copied, n_nat)

                jobs = att_jobs(l)
                J0 = before(att_jobs, l)
                M = len(jobs)
                for s in range(M + 4):
                    if s < M:
                        a = J0 + s
                        b, t, h = jobs[s]
                        if s >= 4:
                            eng.wait_ge(exp_done, a - 3)
                        if b == N:
                            pair, side, kp = h // 2, h % 2, h // 2
                        else:
                            pair, side, kp = h % 4, h // 4, 0
                        part = slice(DH * side, DH * side + DH)
                        w = slice(0, CW) if t < NLAT else slice(SEQ, CW)
                        mm(sbank[a % 4][:, w], qT[b][part, pair, P * t:P * t + P], kT[b][part, kp, w],
                           start=True, stop=True).then_inc(qk_mm, 1)
                    d = s - 3
                    if 0 <= d < M:
                        a = J0 + d
                        b, t, h = jobs[d]
                        ks = range(0, NT) if t < NLAT else range(NLAT, NT)
                        eng.wait_ge(p_norm, a + 1)
                        if a >= 2:
                            eng.wait_ge(pt_copied[a % 2], a // 2)
                        for k in ks:
                            ins = mm(bank[3 + a % 2][:, P * k:P * k + P], probs[a % 4][:, P * k:P * k + P], ident,
                                     start=True, stop=True, is_transpose=True)
                        ins.then_inc(pt_tr, 1)
                    d = s - 4
                    if 0 <= d < M:
                        a = J0 + d
                        b, t, h = jobs[d]
                        g = a // H
                        ks = range(0, NT) if t < NLAT else range(NLAT, NT)
                        eng.wait_ge(pt_copied[a % 2], a // 2 + 1)
                        if h == 0 and g >= 2:
                            eng.wait_ge(o_copied, g - 1)
                        for k in ks:
                            v = vN[:, k, DH * h:DH * h + DH] if b == N else \
                                vAB[:, k, b, DH * (h // 4):DH * (h // 4) + DH]
                            dst = bank[5 + g % 2][DH * (h % 2):DH * (h % 2) + DH, P * (h // 2):P * (h // 2) + P]
                            ins = mm(dst, v, PT[a % 2][:, k], start=(k == ks[0]), stop=(k == NT - 1))
                        ins.then_inc(pv_mm, 1)
                eng.wait_ge(o_copied, (J0 + M) // H)

                for i, (n, half, t) in enumerate(merge_jobs(l)):
                    i += before(merge_jobs, l)
                    wb, wg = arrived((f"wb{n}", l)), arrived((f"g{n}{half}", l))
                    if i >= 2:
                        eng.wait_ge(merged, i - 1)
                    for k in range(KD):
                        ins = mm(bank[i % 2][:, :], HT[:, k, P * t:P * t + P], WR[wg][:, k],
                                 start=(k == 0), stop=(k == KD - 1))
                    ins.then_inc(gate_mm, 1)
                    for k in range(4):
                        ins = mm(bank[2 + i % 2][:, :], qT[n][:, k, P * t:P * t + P],
                                 wdown[wb][:, k, CW * half:CW * half + CW], start=(k == 0), stop=(k == 3))
                    ins.then_inc(branch_mm, 1)

                for t in range(nq):
                    eng.wait_ge(merged, before(merge_jobs, l) + len(merge_jobs(l)) - nq + t + 1)
                    if t >= 2:
                        eng.wait_ge(y_copied, 2 * (NT * l + t - 1))
                    for g in range(2):
                        ins = transposes(Y[:, t, CW * g:CW * g + CW], bank[4 + 2 * (t % 2) + g], 4)
                    ins.then_inc(y_tr, 1)
                def router(t):
                    eng.wait_ge(h_copied, 2 * (NT * (2 * l + 1) + t + 1))
                    for k in range(KD):
                        ins = mm(bank[3][:, NE * t:NE * t + NE], HT[:, k, P * t:P * t + P], wr[:, k],
                                 start=(k == 0), stop=(k == KD - 1))
                    return ins

                for i, (t, half) in enumerate(out_jobs(l)):
                    slot = arrived((f"wo{half}", l))
                    eng.wait_ge(y_copied, 2 * (NT * l + t + 1))
                    if i >= 3:
                        eng.wait_ge(x_att, before(out_jobs, l) + i - 2)
                    for k in range(KD):
                        ins = mm(bank[i % 3][:, :], HT[:, k, P * t:P * t + P], WR[slot][:, k],
                                 start=(k == 0), stop=(k == KD - 1))
                    ins.then_inc(out_mm, 1)
                    if t and half:
                        eng.wait_ge(y_copied, 2 * (NT * l + nq))
                        transpose_h(t - 1)

                eng.wait_ge(const_in, 80)
                for t in range(nq - 1):
                    router(t)
                transpose_h(nq - 1)
                ins = router(nq - 1)
                eng.wait_ge(x_att, before(out_jobs, l) + 2 * nq)
                ins.then_inc(router_mm, 1)
                if l == 0:
                    for i in range(3):
                        modulation(NMOD + i)
                eng.wait_ge(sel_ready, l + 1)
                ones = tabh[:, H_ONE:H_ONE + P]
                for t in range(nq):
                    for t2 in range(t + 1):
                        mm(bank[1][:, NE * t:NE * t + NE], ones if t2 < t else tabh[:, H_PRE:H_PRE + P],
                           selh[:, t2], start=(t2 == 0), stop=(t2 == t))
                for t in range(nq):
                    ins = mm(bank[1][:, NE * nq:NE * nq + NE], ones, selh[:, t], start=(t == 0), stop=(t == nq - 1))
                ins.then_inc(pos_mm, 1)
                if l == 0:
                    modulation(NMOD + 3)
                    modulation(NMOD + 4)
                eng.wait_ge(oneh_ready, NT * l + nq)
                for e in range(NE):
                    for t in range(nq):
                        ins = mm(bank[2][:, e:e + 1], oneh[t][:, P * e:P * e + P], tabh[:, H_TOK + t:H_TOK + t + 1],
                                 start=(t == 0), stop=(t == nq - 1))
                ins.then_inc(idx_mm, 1)
                if l == 0:
                    for i in range(5, MOD_GAP):
                        modulation(NMOD + i)

                base = {s: held[l, s][1] for s in range(SLOTS)}

                def transpose_rows(n, parity, k):
                    eng.wait_ge(hg_in[parity], k)
                    eng.wait_ge(hgT_copied, 2 * n)
                    for g in range(2):
                        ins = transposes(hg[parity][:, CW * g:CW * g + CW], bank[6 + g], 4)
                    ins.then_inc(hg_tr, 1)

                def up_gate(n, parity, k):
                    eng.wait_ge(hgT_copied, 2 * n + 2)
                    for j, (freed, done) in enumerate(((silu_done, eg_mm), (ea_ready, eu_mm))):
                        s = 3 * parity + j
                        eng.wait_ge(w_in_slot[s], base[s] + k)
                        eng.wait_ge(freed, n)
                        for c8 in range(KD):
                            ins = mm(bank[j][:, :], hgT[parity][:, c8], WR[s][:, c8], start=(c8 == 0),
                                     stop=(c8 == KD - 1))
                        ins.then_inc(done, 1)

                def down(n, parity, k):
                    s = 3 * parity + 2
                    eng.wait_ge(w_in_slot[s], base[s] + k)
                    eng.wait_ge(eaT_copied, n + 1)
                    for half, freed in enumerate((yd_lo, yd_hi)):
                        eng.wait_ge(freed, n)
                        for c4 in range(4):
                            ins = mm(bank[4 + half][:, :], eaT[:, c4], wdown[s][:, c4, CW * half:CW * half + CW],
                                     start=(c4 == 0), stop=(c4 == 3))
                        ins.then_inc(ed_mm, 1)

                def transpose_a(n):
                    eng.wait_ge(ea_ready, n + 1)
                    eng.wait_ge(eaT_copied, n)
                    transposes(ea, bank[2], 4).then_inc(ea_tr, 1)

                E0, G0 = NE * l, 16 * (NE // 2) * l
                eng.wait_ge(idx_ready, l + 1)
                transpose_rows(E0, 0, G0 + 16)
                up_gate(E0, 0, 16)
                transpose_rows(E0 + 1, 1, G0 + 16)
                transpose_a(E0)
                def step(n, o, before16):
                    up_gate(n, o % 2, before16 + 16)
                    even = 16 * (1 - o % 2)
                    transpose_rows(n + 1, (o + 1) % 2, G0 + before16 + 32 - even)
                    down(n - 1, (o - 1) % 2, before16 + 16 - even)
                    transpose_a(n)

                step(E0 + 1, 1, 0)
                step(E0 + 2, 2, 16)
                with eng.Fori(0, LOOPS) as i:
                    for o in (3, 4):
                        step(E0 + 2 * i + o, o, 16 * i + 16 * (o // 2))
                up_gate(E0 + NE - 1, 1, 8 * NE)
                down(E0 + NE - 2, 0, 8 * NE)
                transpose_a(E0 + NE - 1)
                down(E0 + NE - 1, 1, 8 * NE)

                eng.wait_ge(flag_ready, l + 1)
                most = eng.value_load(flag[0:1, 0:1], min_val=0, max_val=NT * P)
                with eng.If(most > CAP):
                    q = sp[l]
                    for i in range(2):
                        eng.wait_ge(y_out[i], 16 * (NE // 2) * (l + 1))
                    with eng.Fori(0, (NT - 1) * NE) as n:
                        eng.wait_ge(q["onehot"], n + 1)
                        for t in range(nq):
                            ins = mm(bank[2][:, 0:1], sp_oh[:, t], tabh[:, H_TOK + t:H_TOK + t + 1],
                                     start=(t == 0), stop=(t == nq - 1))
                        ins.then_inc(q["idx_mm"], 1)
                        eng.wait_ge(q["rows_in"], 16 * n + 16)
                        for g in range(2):
                            ins = transposes(hg[0][:, CW * g:CW * g + CW], bank[6 + g], 4)
                        ins.then_inc(q["hg_tr"], 1)
                        eng.wait_ge(q["hgT"], 2 * n + 2)
                        eng.wait_ge(q["w_in"], 48 * n + 48)
                        for j in range(2):
                            for k in range(KD):
                                ins = mm(bank[j][:, :], hgT[0][:, k], WR[j][:, k], start=(k == 0), stop=(k == KD - 1))
                        ins.then_inc(q["up_mm"], 1)
                        eng.wait_ge(q["a"], n + 1)
                        transposes(ea, bank[3], 4).then_inc(q["a_tr"], 1)
                        eng.wait_ge(q["aT"], n + 1)
                        for half in range(2):
                            for k in range(4):
                                ins = mm(bank[4 + half][:, :], eaT[:, k], wdown[2][:, k, CW * half:CW * half + CW],
                                         start=(k == 0), stop=(k == 3))
                        ins.then_inc(q["down_mm"], 1)
                    eng.wait_ge(q["y"], (NT - 1) * NE)
                if l == 0:
                    eng.wait_ge(eaT_copied, NE)
                    for j in range(MOD_GAP, NMOD):
                        modulation(NMOD + j)


def tables():
    import numpy as np
    tab = np.zeros((P, T_COLS), np.float32)
    masks = np.zeros((P, M_COLS), mybir.dt.np(BF16))
    tab[:, T_IDENT:T_IDENT + P] = np.eye(P)
    tok = np.arange(SEQ)
    half = DH // 2
    inv = (np.float32(10000.0) ** (-np.arange(0, half, 2, dtype=np.float32) / np.float32(half))).astype(np.float32)
    ang = np.stack([(tok // GRID_W).astype(np.float32)[:, None] * inv,
                    (tok % GRID_W).astype(np.float32)[:, None] * inv], axis=1).astype(np.float32)
    cos, sin = np.cos(ang), np.sin(ang)
    for t in range(NLAT):
        rows = slice(P * t, P * t + P)
        tab[:, T_ROPEC + DH * t:T_ROPEC + DH * t + DH] = np.stack([cos[rows]] * 2, axis=2).reshape(P, DH)
        tab[:, T_ROPES + DH * t:T_ROPES + DH * t + DH] = np.stack([-sin[rows], sin[rows]], axis=1).reshape(P, DH)
        off = np.abs(tok[None, :] - tok[rows][:, None]) > 128
        masks[:, M_BAND + CW * t:M_BAND + CW * t + SEQ][off] = NEG
    c = np.arange(P) % GRID_W
    lo = np.clip(c - 8, 0, GRID_W - 16)[:, None]
    k = np.arange(GRID_W)[None, :]
    win = np.where((k >= lo) & (k < lo + 16), 0.0, NEG)
    masks[:, M_COLWIN:M_COLWIN + SEQ] = np.tile(win, (1, 4))
    tab[:, T_IOTA:T_IOTA + P] = np.arange(P)
    tab[:, T_RANK:T_RANK + NE] = NE - np.arange(NE)
    tab[:, T_EBASE:T_EBASE + NE] = CAP * np.arange(NE)
    tab[:, T_EPS] = EPS
    tabh = np.zeros((P, H_COLS), np.float16)
    tabh[:, H_PRE:H_PRE + P] = np.arange(P)[:, None] < np.arange(P)[None, :]
    tabh[:, H_ONE:H_ONE + P] = 1
    tabh[:, H_TOK:H_TOK + NT] = np.arange(P)[:, None] + P * np.arange(NT)[None, :]
    return tab, masks, tabh


def kernel(**inputs):
    import numpy as np
    import concourse.bacc as bacc
    from concourse.bass_utils import run_bass_kernel_spmd as run

    arrays = {k: np.ascontiguousarray(v) for k, v in inputs.items() if k != "rpb_n"}
    padded = np.pad(np.asarray(inputs["rpb_n"]), ((0, 0), (0, 0), (0, 0), (48, 48)))
    arrays["rpb"] = np.ascontiguousarray(
        np.lib.stride_tricks.sliding_window_view(padded, GRID_W, axis=-1)[..., ::-1, :])
    arrays["tab"], arrays["masks"], arrays["tabh"] = tables()
    nc = bacc.Bacc("TRN2", target_bir_lowering=False, num_devices=1)
    t_in = {k: nc.dram_tensor(k, v.shape, mybir.dt.from_np(v.dtype), kind="ExternalInput").ap()
            for k, v in arrays.items()}
    out = nc.dram_tensor("out", (1, SEQ, D), F32, kind="ExternalOutput").ap()
    build(nc, t_in, out)
    return run(nc, [arrays], core_ids=[0]).results[0]["out"]
```
